# Optimizing a Trainium2 kernel written in Bass

```python
import math
import jax, jax.numpy as jnp
from jax import lax
import numpy as np

D_MODEL = 1024
BATCH = 1
SEQ = 256
DEPTH = 1

N_META = 16
POOL_WINDOWS = (2, 4, 8, 16)
POOL_GROUPS = 4
POOL_WIDTH = D_MODEL // 2
POOL_GC = POOL_WIDTH // POOL_GROUPS
N_HEADS = 8
HEAD_DIM = 64
N_KV = 2
Q_WIDTH = N_HEADS * HEAD_DIM
KV_WIDTH = N_KV * HEAD_DIM
IDX_HEADS = 4
IDX_DIM = 64
IDX_ROPE = 32
IDX_Q_WIDTH = IDX_HEADS * IDX_DIM
TOPK_CAP = 256
Q_BLOCK = 128
ROPE_THETA = 10000.0
N_KEYS = 128
N_EXPERTS = N_KEYS * N_KEYS
PEER_HEADS = 8
PEER_QDIM = 256
PEER_HALF = PEER_QDIM // 2
PEER_TOPK = 16
PEER_CHUNK = 128
LN_EPS = 1e-5
ALPHA = (2 * DEPTH) ** 0.25
BETA = (8 * DEPTH) ** -0.25

IN_SIZES = (POOL_WIDTH, Q_WIDTH, KV_WIDTH, KV_WIDTH, IDX_Q_WIDTH, IDX_DIM, IDX_HEADS, D_MODEL, D_MODEL)
IN_SPLITS = [sum(IN_SIZES[:i + 1]) for i in range(len(IN_SIZES) - 1)]
IN_WIDTH = sum(IN_SIZES)
V_OFFSET = IN_SPLITS[2]

kernel_name = "hybrid_pool_dsa_peer_deepnorm"

def layer_norm(x, g, b):
    xf = x.astype(jnp.float32)
    mu = jnp.mean(xf, axis=-1, keepdims=True)
    var = jnp.mean(jnp.square(xf - mu), axis=-1, keepdims=True)
    return ((xf - mu) * lax.rsqrt(var + LN_EPS) * g.astype(jnp.float32) + b.astype(jnp.float32)).astype(x.dtype)

def rope(x, pos, rot_dim):
    half = rot_dim // 2
    inv = ROPE_THETA ** (-jnp.arange(half, dtype=jnp.float32) / half)
    ang = pos.astype(jnp.float32)[:, None] * inv[None, :]
    cos = jnp.cos(ang)[None, :, None, :]
    sin = jnp.sin(ang)[None, :, None, :]
    xr = x[..., :rot_dim].astype(jnp.float32)
    x1, x2 = xr[..., :half], xr[..., half:]
    rot = jnp.concatenate([x1 * cos - x2 * sin, x2 * cos + x1 * sin], axis=-1).astype(x.dtype)
    return jnp.concatenate([rot, x[..., rot_dim:]], axis=-1)

def pool_mixer(xp, w_group, scale):
    B, T, _ = xp.shape
    xg = xp.reshape(B, T, POOL_GROUPS, POOL_GC).astype(jnp.float32)
    cs = jnp.cumsum(xg, axis=1)
    t1 = jnp.arange(1, T + 1, dtype=jnp.float32)
    pooled = []
    for g, w in enumerate(POOL_WINDOWS):
        c = cs[:, :, g]
        lag = jnp.pad(c, ((0, 0), (w, 0), (0, 0)))[:, :T]
        cnt = jnp.minimum(t1, float(w))[None, :, None]
        pooled.append((c - lag) / cnt)
    mixed = (jnp.stack(pooled, axis=2) - xg).astype(xp.dtype)
    y = jnp.einsum('btgc,gcd->btgd', mixed, w_group).reshape(B, T, POOL_WIDTH)
    return y * scale

def dsa_attention(q, k, v, qi, ki, wi, topk):
    B, T = q.shape[0], q.shape[1]
    nb = T // Q_BLOCK
    pos = jnp.arange(T)
    q = rope(q, pos, HEAD_DIM)
    k = rope(k, pos, HEAD_DIM)
    qi = rope(qi, pos, IDX_ROPE)
    ki = rope(ki[:, :, None, :], pos, IDX_ROPE)[:, :, 0, :]
    wi = wi * (IDX_HEADS ** -0.5 * IDX_DIM ** -0.5)

    def to_blocks(a):
        return a.reshape(B, nb, Q_BLOCK, *a.shape[2:]).swapaxes(0, 1)

    def block(args):
        qb, qib, wb, qpos = args
        iscore = jax.nn.relu(jnp.einsum('bqhd,bsd->bqhs', qib, ki).astype(jnp.float32))
        isum = jnp.einsum('bqh,bqhs->bqs', wb.astype(jnp.float32), iscore)
        causal = pos[None, None, :] <= qpos[None, :, None]
        isum = jnp.where(causal, isum, -jnp.inf)
        _, idx = lax.top_k(isum, topk)
        valid = idx <= qpos[None, :, None]
        kg = jax.vmap(lambda kb, ib: kb[ib])(k, idx)
        vg = jax.vmap(lambda vb, ib: vb[ib])(v, idx)
        qg = qb.reshape(B, Q_BLOCK, N_KV, N_HEADS // N_KV, HEAD_DIM)
        s = jnp.einsum('bqgrd,bqkgd->bqgrk', qg, kg).astype(jnp.float32) * (HEAD_DIM ** -0.5)
        s = jnp.where(valid[:, :, None, None, :], s, -jnp.inf)
        p = jax.nn.softmax(s, axis=-1).astype(v.dtype)
        o = jnp.einsum('bqgrk,bqkgd->bqgrd', p, vg)
        return o.reshape(B, Q_BLOCK, Q_WIDTH)

    out = lax.map(block, (to_blocks(q), to_blocks(qi), to_blocks(wi), pos.reshape(nb, Q_BLOCK)))
    return out.swapaxes(0, 1).reshape(B, T, Q_WIDTH)

def mixer_block(h, w_in, b_gate, pool_w, pool_scale, w_pool_up, w_attn_o, w_out, topk):
    B, T, _ = h.shape
    z = h @ w_in
    xp, q, k, v, qi, ki, wi, gp, ga = jnp.split(z, IN_SPLITS, axis=-1)
    pool_out = pool_mixer(xp, pool_w, pool_scale) @ w_pool_up
    attn = dsa_attention(q.reshape(B, T, N_HEADS, HEAD_DIM), k.reshape(B, T, N_KV, HEAD_DIM),
                         v.reshape(B, T, N_KV, HEAD_DIM), qi.reshape(B, T, IDX_HEADS, IDX_DIM),
                         ki, wi, topk) @ w_attn_o
    merged = (jax.nn.sigmoid(gp + b_gate[:D_MODEL]) * pool_out
              + jax.nn.sigmoid(ga + b_gate[D_MODEL:]) * attn)
    return merged @ w_out

def peer(h, w_q, sub_keys, u_tab, v_tab):
    B, T, D = h.shape
    n = B * T
    xf = h.reshape(n, D)
    q = (xf @ w_q).reshape(n, PEER_HEADS, 2, PEER_HALF)
    s1 = jnp.einsum('nhd,hkd->nhk', q[:, :, 0], sub_keys[:, 0])
    s2 = jnp.einsum('nhd,hkd->nhk', q[:, :, 1], sub_keys[:, 1])
    v1, i1 = lax.top_k(s1, PEER_TOPK)
    v2, i2 = lax.top_k(s2, PEER_TOPK)
    cand = (v1[..., :, None] + v2[..., None, :]).reshape(n, PEER_HEADS, PEER_TOPK * PEER_TOPK)
    cidx = (i1[..., :, None] * N_KEYS + i2[..., None, :]).reshape(n, PEER_HEADS, PEER_TOPK * PEER_TOPK)
    top, sel = lax.top_k(cand, PEER_TOPK)
    eidx = jnp.take_along_axis(cidx, sel, axis=-1)
    gate = jax.nn.softmax(top.astype(jnp.float32), axis=-1).astype(h.dtype)
    nc = n // PEER_CHUNK

    def chunk(args):
        xc, ec, gc = args
        act = jax.nn.gelu(jnp.einsum('cd,ced->ce', xc, u_tab[ec]), approximate=False)
        return jnp.einsum('ce,ced->cd', gc * act, v_tab[ec])

    y = lax.map(chunk, (xf.reshape(nc, PEER_CHUNK, D),
                        eidx.reshape(nc, PEER_CHUNK, PEER_HEADS * PEER_TOPK),
                        gate.reshape(nc, PEER_CHUNK, PEER_HEADS * PEER_TOPK)))
    return y.reshape(B, T, D)

def setup_inputs(seed: int = 0) -> dict:
    key = jax.random.key(seed)
    ks = jax.random.split(key, 20)
    f32 = jnp.float32
    D = D_MODEL
    nrm = lambda k, shape, s: jax.random.normal(k, shape, f32) * s
    col_scale = jnp.ones((IN_WIDTH,), f32).at[V_OFFSET:V_OFFSET + KV_WIDTH].set(BETA)
    return {
        "x": nrm(ks[0], (BATCH, SEQ, D), 1.0),
        "meta_tokens": nrm(ks[1], (N_META, D), 1.0),
        "ln0_g": 1.0 + nrm(ks[2], (D,), 0.02),
        "ln0_b": nrm(ks[3], (D,), 0.02),
        "w_in": nrm(ks[4], (DEPTH, D, IN_WIDTH), D ** -0.5) * col_scale,
        "b_gate": nrm(ks[5], (DEPTH, 2 * D), 0.02),
        "pool_w": nrm(ks[6], (DEPTH, POOL_GROUPS, POOL_GC, POOL_GC), POOL_GC ** -0.5),
        "pool_scale": 1.0 + nrm(ks[7], (DEPTH, POOL_WIDTH), 0.02),
        "w_pool_up": nrm(ks[8], (DEPTH, POOL_WIDTH, D), POOL_WIDTH ** -0.5 * BETA),
        "w_attn_o": nrm(ks[9], (DEPTH, Q_WIDTH, D), Q_WIDTH ** -0.5 * BETA),
        "w_out": nrm(ks[10], (DEPTH, D, D), D ** -0.5 * BETA),
        "ln1_g": 1.0 + nrm(ks[11], (DEPTH, D), 0.02),
        "ln1_b": nrm(ks[12], (DEPTH, D), 0.02),
        "peer_wq": nrm(ks[13], (DEPTH, D, PEER_HEADS * PEER_QDIM), D ** -0.5),
        "peer_sub_keys": nrm(ks[14], (DEPTH, PEER_HEADS, 2, N_KEYS, PEER_HALF), PEER_HALF ** -0.5),
        "peer_u": nrm(ks[15], (DEPTH, N_EXPERTS, D), D ** -0.5),
        "peer_v": nrm(ks[16], (DEPTH, N_EXPERTS, D), BETA),
        "ln2_g": 1.0 + nrm(ks[17], (DEPTH, D), 0.02),
        "ln2_b": nrm(ks[18], (DEPTH, D), 0.02),
    }

def reference(x, meta_tokens, ln0_g, ln0_b, w_in, b_gate, pool_w, pool_scale, w_pool_up,
              w_attn_o, w_out, ln1_g, ln1_b, peer_wq, peer_sub_keys, peer_u, peer_v, ln2_g, ln2_b):
    B, S, D = x.shape
    T = N_META + S
    T_pad = -(-T // Q_BLOCK) * Q_BLOCK
    meta = jnp.broadcast_to(meta_tokens.astype(x.dtype)[None], (B, N_META, D))
    h = jnp.concatenate([meta, x, jnp.zeros((B, T_pad - T, D), x.dtype)], axis=1)
    h = layer_norm(h, ln0_g, ln0_b)
    topk = min(TOPK_CAP, S // 4)
    for l in range(DEPTH):
        mix = mixer_block(h, w_in[l], b_gate[l], pool_w[l], pool_scale[l], w_pool_up[l],
                          w_attn_o[l], w_out[l], topk)
        h = layer_norm(ALPHA * h + mix, ln1_g[l], ln1_b[l])
        ffn = peer(h, peer_wq[l], peer_sub_keys[l], peer_u[l], peer_v[l])
        h = layer_norm(ALPHA * h + ffn, ln2_g[l], ln2_b[l])
    return h[:, N_META:N_META + S]


_drawn_inputs = setup_inputs


def setup_inputs(seed=0):
    import zlib

    import numpy as np

    out = dict(_drawn_inputs(seed))
    spreads = {}
    factors = {'b_gate': 5.567, 'pool_scale': 3.885, 'ln2_g': 2.869, 'ln2_b': 2.903}
    for name, (base, spread) in spreads.items():
        noise = np.random.default_rng([zlib.crc32(name.encode()), seed]).standard_normal(out[name].shape)
        drawn = base * np.exp(spread * noise) if base else spread * noise
        out[name] = __import__('jax').numpy.asarray(drawn.astype(out[name].dtype))
    for name, factor in factors.items():
        out[name] = (out[name] * factor).astype(out[name].dtype)
    return out
```

```python
from contextlib import ExitStack

import concourse.bass as bass
import numpy as np
from concourse import mybir

ALU = mybir.AluOpType
ACT = mybir.ActivationFunctionType
AX_X = mybir.AxisListType.X
F32 = mybir.dt.float32
U32 = mybir.dt.uint32

P = 128
D = 1024
KD = D // P
N_META = 16
SEQ = 256
NPOS = N_META + SEQ
TILES = 2
PW = 512
PG = 4
WINDOWS = (2, 4, 8, 16)
HEADS, DH, KV = 8, 64, 2
IH = 4
QKVI = HEADS * DH + 2 * KV * DH + IH * DH + DH + IH
OFF_K, OFF_V, OFF_QI, OFF_KI, OFF_WI = 512, 640, 768, 1024, 1088
TOPK = 64
SCALE = DH ** -0.5
PH = 8
EK = 16
NK = 128
LN_EPS = 1e-5
ALPHA = 2.0 ** 0.25
NEG_CAUSAL = -3.0e38
NEG_TAKEN = -3.4e38
MASK = 1.0e30
RING = 8
GRP = 2
GPU = EK // GRP
AHEAD = RING // GRP
UNITS = TILES * PH
TOPK_STEPS = 24
SLOT = 4096
NK_OF = (N_META + P, NPOS)
POS = (N_META, N_META + P)


def bank_jobs():
    jobs = [("hT", t, c) for t in "MAB" for c in range(1 if t == "M" else 2)]
    jobs += [("zk", t) for t in "ABM"] + [("zs", t) for t in "ABM"] + [("zq", t) for t in "AB"]
    jobs += [("xp", g) for g in range(PG)]
    jobs += [("iT", "A"), ("iT", "B"), ("mT",)]
    jobs += [("is", 0, h) for h in range(IH)]
    jobs += [("kT",), ("qT", 0), ("qT", 1)]
    jobs += [("gate", c) for c in range(4)]
    jobs += [("is", 1, h) for h in range(IH)]
    jobs += [("gate", c) for c in range(4, 8)]
    jobs += [("sc", 0, h) for h in range(HEADS)]
    jobs += [("yT", c) for c in range(2)] + [("po", c) for c in range(4)]
    jobs += [("pm", 0, c) for c in range(2)] + [("pk", 0, c) for c in range(2)] + [("pv", 0), ("oT", 0)]
    jobs += [("sc", 1, h) for h in range(HEADS)]
    jobs += [("pm", 1, c) for c in range(2)] + [("pk", 1, c) for c in range(4)] + [("pv", 1), ("oT", 1)]
    jobs += [("ao", c) for c in range(4)]
    jobs += [("mx", t, c) for t in range(TILES) for c in range(2)]
    jobs += [("h1T", t, c) for t in range(TILES) for c in range(2)]
    for c in range(4):
        jobs += [("q2", 2 * c), ("q2", 2 * c + 1), ("ss", 0, c)]
    jobs += [("ss", 1, c) for c in range(4)]
    dve = ("sc", "po", "pv", "ao", "mx")
    return [(j, "dve" if j[0] in dve else "act") for j in jobs]


JOBS = bank_jobs()
JOB_AT = {j: n for n, (j, _) in enumerate(JOBS)}


def taken_before(n, who):
    return sum(w == who for _, w in JOBS[:n])


CHUNKS = [("kvqi", 0), ("q", 1), ("xp", 2), ("g0", 3), ("g1", 4), ("g2", 5), ("g3", 0),
          ("pool_up", 1), ("attn_o", 2), ("out0", 3), ("out1", 0),
          ("wq0", 4), ("wq1", 5), ("wq2", 4), ("wq3", 5)]
LAST_USE = {"kvqi": ("zk", "M"), "q": ("zq", "B"), "xp": ("xp", 3), "g0": ("gate", 1), "g1": ("gate", 3),
            "g2": ("gate", 5), "g3": ("gate", 7), "pool_up": ("po", 3), "attn_o": ("ao", 3),
            "out0": ("mx", 1, 1), "out1": ("mx", 1, 1), "wq0": ("q2", 1), "wq1": ("q2", 3),
            "wq2": ("q2", 5), "wq3": ("q2", 7)}
SLOT_OF = dict(CHUNKS)


def slot_uses(name):
    n = [c for c, _ in CHUNKS].index(name)
    return sum(s == SLOT_OF[name] for _, s in CHUNKS[:n + 1])


def layer_kernel(nc, x, meta, ln, w_in, b_gate_t, pool_w, pool_scale_t, w_pool_up, w_attn_o, w_out,
                 wq, keys_t, uv, rope_q, rope_i, ident_in, alpha_in, iota_in, causal_in, out):
    with ExitStack() as ctx:
        def sb(name, shape, dt=F32):
            return ctx.enter_context(nc.sbuf_tensor(name, shape, dt))

        def sem(name):
            return ctx.enter_context(nc.semaphore(name))

        weights = sb("weights", [P, 6 * SLOT])
        ring = weights[:, 0:4 * SLOT].rearrange("p (s n) -> p s n", s=RING)
        h = sb("h", [P, TILES, D])
        h_meta = weights[0:N_META, 5 * SLOT:5 * SLOT + D]
        hT = sb("hT", [P, KD, NPOS])
        h1T = hT[:, :, 0:SEQ]
        ln_g = sb("ln_g", [P, D])
        ln_b = sb("ln_b", [P, D])
        gT = sb("gT", [P, 2 * KD, SEQ])
        mixed = gT[:, 0:KD, :]
        q2T = gT
        w_small = sb("w_small", [P, KD, 68])
        arena = sb("arena", [P, 7168])
        z = arena[:, 0:2 * QKVI].rearrange("p (t n) -> p t n", t=TILES)
        z_m = arena[:, 2184:2184 + 324]
        r_qk = arena[:, 2508:2508 + 1280].rearrange("p (t h d) -> p t h d", t=TILES, d=DH)
        r_k = arena[:, 3788:3788 + 768].rearrange("p (t g c d) -> p t g c d", t=3, g=KV, c=2)
        r_i = arena[:, 4556:4556 + 1152].rearrange("p (t h d) -> p t h d", t=3, d=DH)
        r_mk = arena[:, 5708:5708 + 128].rearrange("p (h d) -> p h d", d=DH)
        probs = arena[:, 0:HEADS * NPOS].rearrange("p (h n) -> p h n", h=HEADS)
        pT_meta = arena[:, 2176:3200].rearrange("p (h n) -> p h n", h=HEADS)
        pT = arena[:, 3200:5248].rearrange("p (h c n) -> p h c n", h=HEADS, c=2)
        s_all = arena[:, 0:4096].rearrange("p (u n) -> p u n", u=UNITS)
        diag = arena[:, 4096:5120].rearrange("p (s n) -> p s n", s=RING)
        wi = sb("wi", [P, TILES, IH])
        v_sb = sb("v_sb", [P, 3, KV * DH])
        iT = sb("iT", [P, TILES, 2, P])
        kiT = sb("kiT", [P, NPOS])
        qT = sb("qT", [P, TILES, 4, P])
        kT = sb("kT", [P, KV, NPOS])
        rel = sb("rel", [P, IH, NPOS])
        tmp = rel[:, :, :].rearrange("p h n -> p (h n)")
        isum = sb("isum", [P, 2, NPOS])
        causal = sb("causal", [P, TILES, NPOS])
        m8 = sb("m8", [P, 8])
        neg_max = sb("neg_max", [P, HEADS])
        row_sum = sb("row_sum", [P, HEADS])
        row_inv = sb("row_inv", [P, HEADS])
        o_sb = sb("o_sb", [P, HEADS, DH])
        oT = sb("oT", [P, 4, SEQ])
        xpT = sb("xpT", [P, PG, NPOS])
        wsum = sb("wsum", [P, 2, NPOS])
        yT = oT
        pw = sb("pw", [P, PG, P])
        keysT = arena[:, 5120:7168].rearrange("p (c n) -> p c n", c=2 * PH)
        tabs_q = sb("tabs_q", [P, 3, 2, DH])
        tabs_i = sb("tabs_i", [P, 3, 2, 32])
        ident = sb("ident", [P, P])
        alpha_i = sb("alpha_i", [P, P])
        iota16 = sb("iota16", [P, EK])
        bg = sb("bg", [P, 2 * KD])
        ps = sb("ps", [P, PG])
        stats = sb("stats", [P, 2, 6])
        mv = sb("mv", [P, 2])
        nrm = sb("nrm", [P, 8])
        s_cur = tmp[:, 0:512].rearrange("p (u c n) -> p u c n", u=2, c=2)
        s_left = tmp[:, 512:768].rearrange("p (c n) -> p c n", c=2)
        top_v = sb("top_v", [P, 2, EK])
        top_i = sb("top_i", [P, 2, EK], U32)
        top_if = sb("top_if", [P, 2, EK])
        cand = tmp[:, 768:1024].rearrange("p (a b) -> p a b", a=EK)
        cand2 = wsum[:, 0, 0:EK * EK]
        best = sb("best", [P, 2, EK])
        sel = sb("sel", [P, EK], U32)
        ab = sb("ab", [P, 2, EK], U32)
        abf = sb("abf", [P, 2, EK])
        hot = isum[:, :, 0:EK * EK].rearrange("p c (a b) -> p c a b", a=EK)
        pick = sb("pick", [P, 2, EK])
        expert = sb("expert", [P, 2, EK], U32)
        neg_top = sb("neg_top", [P, 2])
        gexp = sb("gexp", [P, 2, EK])
        gsum = sb("gsum", [P, 2])
        ginv = sb("ginv", [P, 2])
        gate = sb("gate", [P, 2, EK])
        dot = sb("dot", [P, 2, EK])
        act_e = sb("act_e", [P, 2, EK])
        w_e = sb("w_e", [P, 2, EK])

        banks = [ctx.enter_context(nc.psum_tensor(f"bank{n}", [P, 512], F32)) for n in range(8)]
        Y = [(banks[4], banks[5]), (banks[6], banks[7])]

        x_in = [sem(f"x_in_{t}") for t in "ABM"]
        ln_in = [sem(f"ln{n}_in") for n in range(3)]
        const_in = sem("const_in")
        small_in = sem("small_in")
        keys_in = sem("keys_in")
        slot_in = [sem(f"slot_in{s}") for s in range(6)]
        bank_full = sem("bank_full")
        bank_taken = {"act": sem("bank_taken_act"), "dve": sem("bank_taken_dve")}
        dve_step = sem("dve_step")
        pool_step = sem("pool_step")
        var_ready = sem("var_ready")
        std_ready = sem("std_ready")
        ln_done = sem("ln_done")
        rotated = sem("rotated")
        rel_used = sem("rel_used")
        scored = sem("scored")
        probs_ready = sem("probs_ready")
        o_ready = sem("o_ready")
        merged = sem("merged")
        windows_done = sem("windows_done")
        s_loaded = sem("s_loaded")
        topk_step = sem("topk_step")
        topk_go = sem("topk_go")
        idx_ready = sem("idx_ready")
        top_ready = sem("top_ready")
        gexp_ready = sem("gexp_ready")
        ginv_ready = sem("ginv_ready")
        gate_ready = sem("gate_ready")
        landed = [sem(f"landed{s}") for s in range(RING)]
        gather_go = sem("gather_go")
        act_go = sem("act_go")
        dots_ready = sem("dots_ready")
        gelu_ready = sem("gelu_ready")
        w_ready = sem("w_ready")
        diag_ready = sem("diag_ready")
        group_free = sem("group_free")
        y_ready = sem("y_ready")
        out_done = sem("out_done")

        def bank(*job):
            return banks[JOB_AT[job] % 8]

        def wait_free(pe, *job):
            n = JOB_AT[job] - 8
            if n >= 0:
                who = JOBS[n][1]
                pe.wait_ge(bank_taken[who], taken_before(n, who) + 1)

        def wait_full(eng, *job):
            eng.wait_ge(bank_full, JOB_AT[job] + 1)

        def wait_taken(eng, *job):
            n = JOB_AT[job]
            who = JOBS[n][1]
            eng.wait_ge(bank_taken[who], taken_before(n, who) + 1)

        def chunk(name, k):
            s = SLOT_OF[name]
            return weights[:, s * SLOT:(s + 1) * SLOT].rearrange("p (k n) -> p k n", k=k)

        def wait_chunk(pe, name):
            pe.wait_ge(slot_in[SLOT_OF[name]], 16 * slot_uses(name))

        rows = {"A": (0, P), "B": (1, P), "M": (2, N_META)}
        where = {"M": 0, "A": POS[0], "B": POS[1]}
        w_in_k = w_in.rearrange("(k p) n -> p k n", p=P)
        SRC = {
            "kvqi": w_in_k[:, :, PW + OFF_K:PW + OFF_K + 512], "q": w_in_k[:, :, PW:PW + 512],
            "xp": w_in_k[:, :, 0:PW],
            **{f"g{c}": w_in_k[:, :, PW + QKVI + 512 * c:PW + QKVI + 512 * c + 512] for c in range(4)},
            "pool_up": w_pool_up.rearrange("(k p) n -> p k n", p=P),
            "attn_o": w_attn_o.rearrange("(k p) n -> p k n", p=P),
            **{f"out{c}": w_out.rearrange("(k p) n -> p k n", p=P)[:, :, 512 * c:512 * c + 512] for c in range(2)},
            **{f"wq{c}": wq.rearrange("(k p) n -> p k n", p=P)[:, :, 512 * c:512 * c + 512] for c in range(4)},
        }

        block = ctx.enter_context(nc.Block())

        @block.sync
        def _(sp):
            def load_ln(n):
                sp.dma_start(ln_g[:, :], ln[2 * n:2 * n + 1, :].partition_broadcast(P)).then_inc(ln_in[n], 16)
                sp.dma_start(ln_b[:, :], ln[2 * n + 1:2 * n + 2, :].partition_broadcast(P)).then_inc(ln_in[n], 16)

            def load_chunk(n):
                name, s = CHUNKS[n]
                if s == 5:
                    wait_full(sp, "hT", "M", 0)
                older = [c for c, t in CHUNKS[:n] if t == s]
                if older:
                    wait_full(sp, *LAST_USE[older[-1]])
                k = SRC[name].shape[1]
                sp.dma_start(chunk(name, k), SRC[name]).then_inc(slot_in[s], 16)

            sp.dma_start(h[:, 0, :], x[0:P, :]).then_inc(x_in[0], 16)
            load_ln(0)
            sp.dma_start(h_meta, meta).then_inc(x_in[2], 16)
            sp.dma_start(h[:, 1, :], x[P:SEQ, :]).then_inc(x_in[1], 16)
            sp.dma_start(ident[:, :], ident_in).then_inc(const_in, 16)
            for t, (n, rows_) in rows.items():
                r = where[t]
                sp.dma_start(tabs_q[0:rows_, n, :, :], rope_q[r:r + rows_]).then_inc(const_in, 16)
                sp.dma_start(tabs_i[0:rows_, n, :, :], rope_i[r:r + rows_]).then_inc(const_in, 16)
            sp.dma_start(causal[:, :, :], causal_in.rearrange("(t p) n -> p t n", p=P)).then_inc(const_in, 16)
            sp.dma_start(bg[:, :], b_gate_t).then_inc(const_in, 16)
            sp.dma_start(ps[:, :], pool_scale_t).then_inc(const_in, 16)
            sp.dma_start(iota16[:, :], iota_in).then_inc(const_in, 16)
            sp.dma_start(alpha_i[:, :], alpha_in).then_inc(const_in, 16)
            load_chunk(0)
            sp.dma_start(w_small[:, :, :], w_in_k[:, :, PW + OFF_KI:PW + QKVI]).then_inc(small_in, 16)
            load_chunk(1)
            load_chunk(2)
            sp.dma_start(pw[:, :, :], pool_w.rearrange("g c d -> c g d")).then_inc(small_in, 16)
            for n in range(3, 7):
                load_chunk(n)
            sp.wait_ge(ln_done, 3)
            load_ln(1)
            for n in range(7, len(CHUNKS)):
                if CHUNKS[n][0] == "wq2":
                    wait_full(sp, "pv", 1)
                    sp.dma_start(keysT[:, :, :], keys_t).then_inc(keys_in, 16)
                load_chunk(n)
            sp.wait_ge(ln_done, 5)
            load_ln(2)
            for t in range(TILES):
                sp.wait_ge(ln_done, 6 + t)
                sp.dma_start(out[0, t * P:(t + 1) * P, :], h[:, t, :]).then_inc(out_done, 16)
            sp.wait_ge(out_done, 16 * TILES)

        N_CONST = 12

        @block.gpsimd
        def _(pool):
            steps = 0
            for g, w in enumerate(WINDOWS):
                wait_taken(pool, "xp", g)
                src, width, first = xpT[:, g, :], 1, 0
                n = 0
                while width < w:
                    first += width
                    dst = wsum[:, n % 2, :]
                    pool.tensor_tensor(dst[:, first:NPOS], src[:, first:NPOS], src[:, first - width:NPOS - width],
                                       ALU.add).then_inc(pool_step, 1)
                    steps += 1
                    pool.wait_ge(pool_step, steps)
                    src, width, n = dst, 2 * width, n + 1
                pool.tensor_scalar(src[:, N_META:NPOS], src[:, N_META:NPOS], 1.0 / w, None, ALU.mult).then_inc(pool_step, 1)
                steps += 1
                pool.wait_ge(pool_step, steps)
                pool.tensor_tensor(xpT[:, g, N_META:NPOS], src[:, N_META:NPOS], xpT[:, g, N_META:NPOS],
                                   ALU.subtract).then_inc(windows_done, 1)
                pool.wait_ge(windows_done, g + 1)

            wait_full(pool, "mx", 1, 1)

            def gather_unit(u, b):
                pool.wait_ge(idx_ready, u + 1)
                for e in range(EK):
                    if e % GRP == 0:
                        pool.wait_ge(group_free, u * GPU + e // GRP + 1)
                        pool.sem_inc(gather_go, 1)
                    pool.indirect_dma_start(ring[:, e % RING, :], None, uv,
                                            bass.IndirectOffsetOnAxis(ap=expert[:, b, e:e + 1], axis=0)
                                            ).then_inc(landed[e % RING], 16)

            with pool.Fori(0, UNITS // 2) as j:
                for b in range(2):
                    gather_unit(2 * j + b, b)

        @block.scalar
        def _(act):
            def take(dst, src, last=True, **kw):
                i = act.activation(dst, src, kw.pop("func", ACT.Copy), **kw)
                if last:
                    i.then_inc(bank_taken["act"], 1)
                return i

            def std(n):
                act.wait_ge(var_ready, n)
                act.activation(nrm[:, 1:2], nrm[:, 0:1], ACT.Sqrt).then_inc(std_ready, 1)

            lns = 0
            for t in "MAB":
                lns += 1
                std(lns)
            for t in "MAB":
                n, r = rows[t]
                for c in range(1 if t == "M" else 2):
                    wait_full(act, "hT", t, c)
                    kk = KD if t == "M" else 4
                    take(hT[:, c * 4:c * 4 + kk, where[t]:where[t] + r],
                         bank("hT", t, c)[:, 0:kk * r].rearrange("p (k n) -> p k n", k=kk))
            for t in "ABM":
                n, r = rows[t]
                wait_full(act, "zk", t)
                src = bank("zk", t)
                take(v_sb[0:r, n, :], src[0:r, 128:256], last=False)
                if t == "M":
                    take(z_m[0:r, 0:256], src[0:r, 0:256])
                else:
                    take(z[:, n, OFF_K:OFF_K + 512], src[:, :])
            for t in "ABM":
                n, r = rows[t]
                wait_full(act, "zs", t)
                src = bank("zs", t)
                if t == "M":
                    take(z_m[0:r, 256:320], src[0:r, 0:64])
                else:
                    take(wi[:, n, :], src[:, 64:68], last=False, scale=IH ** -0.5 * DH ** -0.5)
                    take(z[:, n, OFF_KI:QKVI], src[:, 0:68])
            for t in "AB":
                wait_full(act, "zq", t)
                take(z[:, rows[t][0], 0:512], bank("zq", t)[:, :])
            for g in range(PG):
                wait_full(act, "xp", g)
                take(xpT[:, g, :], bank("xp", g)[:, 0:NPOS])

            def take_relu(t):
                for hd in range(IH):
                    wait_full(act, "is", t, hd)
                    if t == 1 and hd == 0:
                        act.wait_ge(rel_used, 1)
                    take(rel[:, hd, 0:NK_OF[t]], bank("is", t, hd)[:, 0:NK_OF[t]], func=ACT.Relu)

            for t in "AB":
                n, _ = rows[t]
                wait_full(act, "iT", t)
                src = bank("iT", t)
                take(iT[:, n, :, :], src[:, 0:2 * P].rearrange("p (c n) -> p c n", c=2), last=False)
                take(kiT[:, where[t]:where[t] + P], src[:, 2 * P:3 * P])
            wait_full(act, "mT")
            src = bank("mT")
            take(kiT[:, 0:N_META], src[:, 0:N_META], last=False)
            take(kT[:, :, 0:N_META], src[:, N_META:3 * N_META].rearrange("p (g n) -> p g n", g=KV))
            act.wait_ge(rotated, 5)
            take_relu(0)
            wait_full(act, "kT")
            for t in range(TILES):
                take(kT[:, :, POS[t]:POS[t] + P],
                     bank("kT")[:, t * 256:t * 256 + 256].rearrange("p (g n) -> p g n", g=KV), last=(t == 1))
            for t in range(TILES):
                wait_full(act, "qT", t)
                take(qT[:, t, :, :], bank("qT", t)[:, :].rearrange("p (c n) -> p c n", c=4))

            def take_gates(c):
                wait_full(act, "gate", c)
                for i in range(2):
                    take(gT[:, 2 * c + i, :], bank("gate", c)[:, i * SEQ:(i + 1) * SEQ], func=ACT.Sigmoid,
                         bias=bg[:, 2 * c + i:2 * c + i + 1], last=(i == 1))

            act.wait_ge(const_in, 16 * N_CONST)
            for c in range(4):
                take_gates(c)
            take_relu(1)
            for c in range(4, 8):
                take_gates(c)
            for c in range(2):
                wait_full(act, "yT", c)
                for i in range(2):
                    g = 2 * c + i
                    take(yT[:, g, :], bank("yT", c)[:, i * SEQ:(i + 1) * SEQ], scale=ps[:, g:g + 1], last=(i == 1))

            for t in range(TILES):
                for hd in range(HEADS):
                    act.wait_ge(scored, t * HEADS + hd + 1)
                    act.activation(probs[:, hd, 0:NK_OF[t]], probs[:, hd, 0:NK_OF[t]], ACT.Exp,
                                   bias=neg_max[:, hd:hd + 1], scale=-1.0,
                                   accum_out=row_sum[:, hd:hd + 1]).then_inc(probs_ready, 1)
                for c in range(2):
                    wait_full(act, "pm", t, c)
                    take(pT_meta[0:N_META, 4 * c:4 * c + 4, :],
                         bank("pm", t, c)[0:N_META, :].rearrange("p (h n) -> p h n", h=4))
                for c in range(2 * (t + 1)):
                    wait_full(act, "pk", t, c)
                    if t == 0:
                        take(pT[:, 4 * c:4 * c + 4, 0, :], bank("pk", t, c)[:, :].rearrange("p (h n) -> p h n", h=4))
                    else:
                        take(pT[:, 2 * c:2 * c + 2, :, :],
                             bank("pk", t, c)[:, :].rearrange("p (h c n) -> p h c n", h=2, c=2))
                wait_full(act, "oT", t)
                take(oT[:, :, t * P:(t + 1) * P], bank("oT", t)[:, :].rearrange("p (c n) -> p c n", c=4))
            for t in range(TILES):
                lns += 1
                std(lns)
            for t in range(TILES):
                for c in range(2):
                    wait_full(act, "h1T", t, c)
                    take(h1T[:, 4 * c:4 * c + 4, t * P:(t + 1) * P],
                         bank("h1T", t, c)[:, :].rearrange("p (k n) -> p k n", k=4))

            def take_q2(c):
                for n in (2 * c, 2 * c + 1):
                    wait_full(act, "q2", n)
                    take(q2T[:, 2 * n:2 * n + 2, :], bank("q2", n)[:, :].rearrange("p (c n) -> p c n", c=2))

            def take_ss(t, c):
                wait_full(act, "ss", t, c)
                take(s_all[:, t * PH + 2 * c:t * PH + 2 * c + 2, :],
                     bank("ss", t, c)[:, :].rearrange("p (u n) -> p u n", u=2))

            def exp_gates(u, b):
                act.wait_ge(top_ready, u + 1)
                act.activation(gexp[:, b, :], best[:, b, :], ACT.Exp, bias=neg_top[:, b:b + 1],
                               accum_out=gsum[:, b:b + 1]).then_inc(gexp_ready, 1)

            def load_scores(u, b):
                act.activation(s_cur[:, b, :, :].rearrange("p c n -> p (c n)"), s_all[:, u, :],
                               ACT.Copy).then_inc(s_loaded, 1)

            take_q2(0)
            take_ss(0, 0)
            wait_taken(act, "ss", 0, 0)
            for b in range(2):
                load_scores(b, b)
            take_q2(1)
            take_ss(0, 1)
            for b in range(2):
                exp_gates(b, b)
            for c in range(2, 4):
                take_q2(c)
                take_ss(0, c)
            for c in range(4):
                take_ss(1, c)
            wait_taken(act, "ss", 1, 3)

            def diagonals(u, b, g):
                act.wait_ge(group_free, u * GPU + g + 1)
                act.wait_ge(w_ready, u * GPU + g + 1)
                for i in range(GRP):
                    e = g * GRP + i
                    d = act.activation(diag[:, e % RING, :], ident[:, :], ACT.Copy, scale=w_e[:, b, e:e + 1])
                d.then_inc(diag_ready, 1)

            def unit(u, b, nxt):
                if nxt:
                    act.wait_ge(top_ready, u + 1)
                    act.sem_inc(act_go, 1)
                    load_scores(u + 2, b)
                for g in range(GPU):
                    act.wait_ge(dots_ready, u * GPU + g + 1)
                    act.activation(act_e[:, b, g * GRP:(g + 1) * GRP], dot[:, b, g * GRP:(g + 1) * GRP],
                                   ACT.Gelu).then_inc(gelu_ready, 1)
                    if g:
                        diagonals(u, b, g - 1)
                diagonals(u, b, GPU - 1)
                if nxt:
                    exp_gates(u + 2, b)

            with act.Fori(0, 4) as j:
                for b in range(2):
                    unit(2 * j + b, b, True)
            lns += 1
            std(lns)
            with act.Fori(4, 7) as j:
                for b in range(2):
                    unit(2 * j + b, b, True)
            for b in range(2):
                unit(UNITS - 2 + b, b, False)
            lns += 1
            std(lns)

        @block.tensor
        def _(pe):
            def full(mm):
                mm.then_inc(bank_full, 1)

            pe.wait_ge(const_in, 16 * N_CONST)
            for m, t in enumerate("MAB"):
                n, r = rows[t]
                src = h_meta if t == "M" else h[:, n, :]
                pe.wait_ge(ln_done, m + 1)
                for c in range(1 if t == "M" else 2):
                    wait_free(pe, "hT", t, c)
                    kk = KD if t == "M" else 4
                    for k in range(kk):
                        mm = pe.transpose(bank("hT", t, c)[:, k * r:(k + 1) * r],
                                          src[:, (4 * c + k) * P:(4 * c + k + 1) * P], ident[0:r, 0:r])
                    full(mm)

            def project(job, t, w, cols):
                n, r = rows[t]
                wait_free(pe, *job)
                for k in range(KD):
                    mm = pe.matmul(bank(*job)[0:r, 0:cols], hT[:, k, where[t]:where[t] + r], w[:, k, 0:cols],
                                   start=(k == 0), stop=(k == KD - 1))
                full(mm)

            wait_taken(pe, "hT", "B", 1)
            wait_chunk(pe, "kvqi")
            for t in "ABM":
                project(("zk", t), t, chunk("kvqi", KD), 256 if t == "M" else 512)
            pe.wait_ge(small_in, 32)
            for t in "ABM":
                project(("zs", t), t, w_small, 64 if t == "M" else 68)
            wait_chunk(pe, "q")
            for t in "AB":
                project(("zq", t), t, chunk("q", KD), 512)
            wait_chunk(pe, "xp")
            for g in range(PG):
                wait_free(pe, "xp", g)
                for k in range(KD):
                    mm = pe.matmul(bank("xp", g)[:, 0:NPOS], chunk("xp", KD)[:, k, g * P:(g + 1) * P], hT[:, k, :],
                                   start=(k == 0), stop=(k == KD - 1))
                full(mm)

            def transposes(job, srcs, r=P):
                wait_free(pe, *job)
                for i, s in enumerate(srcs):
                    mm = pe.transpose(bank(*job)[:, i * r:(i + 1) * r], s, ident[0:r, 0:r])
                full(mm)

            for m, t in enumerate("AB"):
                n = rows[t][0]
                pe.wait_ge(rotated, m + 1)
                transposes(("iT", t), [r_i[:, n, 2 * c:2 * c + 2, :].rearrange("p h d -> p (h d)") for c in range(3)])
            pe.wait_ge(rotated, 3)
            M = N_META
            transposes(("mT",), [r_i[0:M, 2, 4:6, :].rearrange("p h d -> p (h d)")]
                       + [r_k[0:M, 2, g, :, :].rearrange("p c d -> p (c d)") for g in range(KV)], M)

            def index_scores(t):
                for hd in range(IH):
                    half = slice(64 * (hd % 2), 64 * (hd % 2) + 64)
                    wait_free(pe, "is", t, hd)
                    if hd == 0 and t == 0:
                        wait_taken(pe, "mT")
                    full(pe.matmul(bank("is", t, hd)[:, 0:NK_OF[t]], iT[half, t, hd // 2, :],
                                   kiT[half, 0:NK_OF[t]], start=True, stop=True))

            index_scores(0)
            pe.wait_ge(rotated, 5)
            transposes(("kT",), [r_k[:, t, g, :, :].rearrange("p c d -> p (c d)") for t in range(TILES) for g in range(KV)])
            for t in range(TILES):
                transposes(("qT", t), [r_qk[:, t, 2 * c:2 * c + 2, :].rearrange("p h d -> p (h d)") for c in range(4)])

            def gates(c):
                name = f"g{c // 2}"
                wait_chunk(pe, name)
                wait_free(pe, "gate", c)
                for i in range(2):
                    col = (2 * (c % 2) + i) * P
                    for k in range(KD):
                        mm = pe.matmul(bank("gate", c)[:, i * SEQ:(i + 1) * SEQ], chunk(name, KD)[:, k, col:col + P],
                                       hT[:, k, N_META:NPOS], start=(k == 0), stop=(k == KD - 1))
                full(mm)

            for c in range(4):
                gates(c)
            index_scores(1)
            for c in range(4, 8):
                gates(c)

            def attention_scores(t):
                for hd in range(HEADS):
                    half = slice(64 * (hd % 2), 64 * (hd % 2) + 64)
                    wait_free(pe, "sc", t, hd)
                    if hd == 0 and t == 0:
                        wait_taken(pe, "qT", 1)
                    full(pe.matmul(bank("sc", t, hd)[:, 0:NK_OF[t]], qT[half, t, hd // 2, :],
                                   kT[half, hd // 4, 0:NK_OF[t]], start=True, stop=True))

            def attend(t):
                for c in range(2):
                    pe.wait_ge(probs_ready, t * HEADS + 4 * c + 4)
                    wait_free(pe, "pm", t, c)
                    for i in range(4):
                        mm = pe.transpose(bank("pm", t, c)[0:N_META, i * P:(i + 1) * P],
                                          probs[:, 4 * c + i, 0:N_META], ident[:, :])
                    full(mm)
                per = 4 // (t + 1)
                for c in range(2 * (t + 1)):
                    wait_free(pe, "pk", t, c)
                    for i in range(per):
                        for b in range(t + 1):
                            mm = pe.transpose(bank("pk", t, c)[:, (i * (t + 1) + b) * P:(i * (t + 1) + b + 1) * P],
                                              probs[:, c * per + i, POS[b]:POS[b] + P], ident[:, :])
                    full(mm)
                wait_free(pe, "pv", t)
                wait_taken(pe, "pk", t, 2 * (t + 1) - 1)
                for hd in range(HEADS):
                    g = slice(64 * (hd // 4), 64 * (hd // 4) + 64)
                    o = bank("pv", t)[:, hd * DH:(hd + 1) * DH]
                    pe.matmul(o, pT_meta[0:N_META, hd, :], v_sb[0:N_META, 2, g], start=True, stop=False)
                    for b in range(t + 1):
                        mm = pe.matmul(o, pT[:, hd, b, :], v_sb[:, b, g], start=False, stop=(b == t))
                full(mm)
                pe.wait_ge(o_ready, t + 1)
                transposes(("oT", t), [o_sb[:, 2 * c:2 * c + 2, :].rearrange("p h d -> p (h d)") for c in range(4)])

            def up(job, w, src, c):
                wait_free(pe, *job)
                for i in range(2):
                    col = (2 * c + i) * P
                    for k in range(4):
                        mm = pe.matmul(bank(*job)[:, i * SEQ:(i + 1) * SEQ], w[:, k, col:col + P], src[:, k, :],
                                       start=(k == 0), stop=(k == 3))
                full(mm)

            attention_scores(0)
            pe.wait_ge(windows_done, PG)
            for c in range(2):
                wait_free(pe, "yT", c)
                for i in range(2):
                    g = 2 * c + i
                    mm = pe.matmul(bank("yT", c)[:, i * SEQ:(i + 1) * SEQ], pw[:, g, :], xpT[:, g, N_META:NPOS],
                                   start=True, stop=True)
                full(mm)
            wait_chunk(pe, "pool_up")
            wait_taken(pe, "yT", 1)
            for c in range(4):
                up(("po", c), chunk("pool_up", 4), yT, c)
            attend(0)
            attention_scores(1)
            attend(1)
            wait_chunk(pe, "attn_o")
            wait_taken(pe, "oT", 1)
            for c in range(4):
                up(("ao", c), chunk("attn_o", 4), oT, c)
            for c in range(2):
                wait_chunk(pe, f"out{c}")
            pe.wait_ge(merged, 4)
            for t in range(TILES):
                for c in range(2):
                    wait_free(pe, "mx", t, c)
                    for k in range(KD):
                        mm = pe.matmul(bank("mx", t, c)[:, :], mixed[:, k, t * P:(t + 1) * P], chunk(f"out{c}", KD)[:, k, :],
                                       start=(k == 0), stop=(k == KD - 1))
                    full(mm)
            for t in range(TILES):
                pe.wait_ge(ln_done, 4 + t)
                for c in range(2):
                    transposes(("h1T", t, c), [h[:, t, (4 * c + k) * P:(4 * c + k + 1) * P] for k in range(4)])

            def key_scores(t, c):
                wait_free(pe, "ss", t, c)
                wait_taken(pe, "q2", 2 * c + 1)
                for i in range(4):
                    n = 4 * c + i
                    mm = pe.matmul(bank("ss", t, c)[:, i * NK:(i + 1) * NK], q2T[:, n, t * P:(t + 1) * P], keysT[:, n, :],
                                   start=True, stop=True)
                full(mm)

            wait_taken(pe, "h1T", 1, 1)
            pe.wait_ge(keys_in, 16)
            for c in range(4):
                wait_chunk(pe, f"wq{c}")
                for n in (2 * c, 2 * c + 1):
                    wait_free(pe, "q2", n)
                    for i in range(2):
                        col = (2 * (n % 2) + i) * P
                        for k in range(KD):
                            mm = pe.matmul(bank("q2", n)[:, i * SEQ:(i + 1) * SEQ], chunk(f"wq{c}", KD)[:, k, col:col + P],
                                           h1T[:, k, :], start=(k == 0), stop=(k == KD - 1))
                    full(mm)
                key_scores(0, c)
            for c in range(4):
                key_scores(1, c)
            wait_taken(pe, "ss", 1, 3)

            for t in range(TILES):
                for c in range(2):
                    pe.matmul(Y[t][c][:, :], alpha_i[:, :], h[:, t, c * 512:(c + 1) * 512], start=True, stop=False,
                              skip_group_check=True)
            pe.sem_inc(group_free, AHEAD)

            def unit(u, t, final):
                for g in range(GPU):
                    pe.wait_ge(diag_ready, u * GPU + g + 1)
                    for i in range(GRP):
                        s = (g * GRP + i) % RING
                        for c in range(2):
                            last = final and g == GPU - 1 and i == GRP - 1
                            mm = pe.matmul(Y[t][c][:, :], diag[:, s, :], ring[:, s, D + c * 512:D + (c + 1) * 512],
                                           start=False, stop=last, skip_group_check=True)
                    mm.then_inc(group_free, 1)

            with pe.Fori(0, 4) as j:
                for b in range(2):
                    unit(2 * j + b, 0, False)
            with pe.Fori(4, 8) as j:
                for b in range(2):
                    unit(2 * j + b, 1, False)

        @block.vector
        def _(v):
            count = [0, 0]

            def link(i):
                count[0] += 1
                i.then_inc(dve_step, 1)
                v.wait_ge(dve_step, count[0])

            def step(i):
                count[0] += 1
                i.then_inc(dve_step, 1)

            def sync():
                v.wait_ge(dve_step, count[0])

            def layer_norm(dst, halves, r):
                for c in range(2):
                    step(v.bn_stats(stats[0:r, c, :], halves[c]))
                sync()
                link(v.bn_aggr(mv[0:r, :], stats[0:r, :, :].rearrange("p c n -> p (c n)")))
                v.tensor_scalar(nrm[0:r, 0:1], mv[0:r, 1:2], LN_EPS, None, ALU.add).then_inc(var_ready, 1)
                for c in range(2):
                    step(v.scalar_tensor_tensor(dst[:, c * 512:(c + 1) * 512], halves[c], mv[0:r, 0:1],
                                                ln_g[0:r, c * 512:(c + 1) * 512], ALU.subtract, ALU.mult))
                count[1] += 1
                v.wait_ge(std_ready, count[1])
                link(v.reciprocal(nrm[0:r, 2:3], nrm[0:r, 1:2]))
                link(v.tensor_scalar(nrm[0:r, 3:4], nrm[0:r, 2:3], nrm[0:r, 2:3], nrm[0:r, 0:1], ALU.mult, ALU.mult))
                link(v.tensor_scalar(nrm[0:r, 4:5], nrm[0:r, 3:4], -0.5, 1.5, ALU.mult, ALU.add))
                link(v.tensor_scalar(nrm[0:r, 5:6], nrm[0:r, 4:5], nrm[0:r, 2:3], None, ALU.mult))
                v.scalar_tensor_tensor(dst[:, :], dst[:, :], nrm[0:r, 5:6], ln_b[0:r, :], ALU.mult,
                                       ALU.add).then_inc(ln_done, 1)
                v.wait_ge(ln_done, count[1])

            link(v.memset(nrm[:, :], 1.0))
            v.wait_ge(ln_in[0], 32)
            for t in "MAB":
                n, r = rows[t]
                v.wait_ge(x_in[n], 16)
                src = h_meta if t == "M" else h[:, n, :]
                layer_norm(src, [src[:, 0:512], src[:, 512:1024]], r)

            def rope(src, dst, tab, r, hh, half):
                w = 2 * half
                t2 = tmp[0:r, 0:hh * w].rearrange("p (h d) -> p h d", h=hh)
                cos = tab[:, 0, :].unsqueeze(1).broadcast_to([r, hh, w])
                sin = tab[:, 1, :].unsqueeze(1).broadcast_to([r, hh, w])
                step(v.tensor_tensor(dst[:, :, 0:w], src[:, :, 0:w], cos, ALU.mult))
                step(v.tensor_tensor(t2[:, :, 0:half], src[:, :, half:w], sin[:, :, 0:half], ALU.mult))
                link(v.tensor_tensor(t2[:, :, half:w], src[:, :, 0:half], sin[:, :, half:w], ALU.mult))
                link(v.tensor_tensor(dst[:, :, 0:w], dst[:, :, 0:w], t2, ALU.add))

            v.wait_ge(const_in, 16 * N_CONST)

            def rope_index(n, r, src):
                hh = src.shape[1]
                dst = r_i[0:r, n, 5 - hh:5, :]
                step(v.tensor_copy(dst[:, :, 32:64], src[:, :, 32:64]))
                rope(src, dst, tabs_i[0:r, n, :, :], r, hh, 16)
                return v.tensor_copy(r_i[0:r, n, 5, :], r_i[0:r, n, 4, :])

            for m, t in enumerate("AB"):
                n, r = rows[t]
                wait_taken(v, "zs", t)
                rope_index(n, r, z[:, n, OFF_QI:OFF_QI + 320].rearrange("p (h d) -> p h d", d=DH)).then_inc(rotated, 1)
                v.wait_ge(rotated, m + 1)
            wait_taken(v, "zs", "M")
            M = N_META
            link(rope_index(2, M, z_m[0:M, 256:320].rearrange("p (h d) -> p h d", d=DH)))
            rope(z_m[0:M, 0:128].rearrange("p (h d) -> p h d", d=DH), r_mk[0:M, :, :], tabs_q[0:M, 2, :, :], M, KV, 32)
            v.tensor_copy(r_k[0:M, 2, :, :, :], r_mk[0:M, :, :].unsqueeze(2).broadcast_to([M, KV, 2, DH])).then_inc(rotated, 1)
            v.wait_ge(rotated, 3)
            for m, t in enumerate("AB"):
                n, r = rows[t]
                wait_taken(v, "zq", t)
                rope(z[:, n, 0:640].rearrange("p (h d) -> p h d", d=DH), r_qk[:, n, :, :], tabs_q[:, n, :, :], r, 10, 32)
                v.tensor_copy(r_k[:, n, :, :, :], r_qk[:, n, 8:10, :].unsqueeze(2).broadcast_to([P, KV, 2, DH])).then_inc(rotated, 1)
                v.wait_ge(rotated, 4 + m)

            def select_keys(t):
                n = NK_OF[t]
                acc, left = isum[:, 0, 0:n], isum[:, 1, 0:n]
                mask = causal[:, t, 0:n]
                src = mask
                for hd in range(IH):
                    wait_taken(v, "is", t, hd)
                    i = v.scalar_tensor_tensor(acc, rel[:, hd, 0:n], wi[:, t, hd:hd + 1], src if hd == 0 else acc,
                                               ALU.mult, ALU.add) if hd else \
                        v.tensor_scalar(acc, rel[:, 0, 0:n], wi[:, t, 0:1], None, ALU.mult)
                    if hd == IH - 1:
                        i.then_inc(rel_used, 1)
                        v.wait_ge(rel_used, t + 1)
                    else:
                        link(i)
                link(v.tensor_tensor(acc, acc, mask, ALU.add))
                cur, other = acc, left
                for _ in range(TOPK // 8):
                    link(v.max(m8[:, :], cur))
                    link(v.match_replace(other, m8[:, :], cur, NEG_TAKEN))
                    cur, other = other, cur
                link(v.tensor_scalar(cur, cur, -3.2e38, MASK, ALU.is_le, ALU.mult))
                link(v.tensor_scalar(mask, mask, -MASK / NEG_CAUSAL, -MASK, ALU.mult, ALU.add))
                link(v.tensor_tensor(mask, mask, cur, ALU.add))

            def softmax_inputs(t):
                n = NK_OF[t]
                if t == 0:
                    wait_full(v, "qT", 1)
                else:
                    wait_full(v, "pk", 0, 1)
                    v.wait_ge(o_ready, 1)
                for hd in range(HEADS):
                    wait_full(v, "sc", t, hd)
                    v.tensor_tensor_reduce(probs[:, hd, 0:n], bank("sc", t, hd)[:, 0:n], causal[:, t, 0:n], -SCALE, 3.0e38,
                                           ALU.add, ALU.min, neg_max[:, hd:hd + 1]).then_inc(bank_taken["dve"], 1)
                    wait_taken(v, "sc", t, hd)
                    v.sem_inc(scored, 1)

            def normalise(t):
                v.wait_ge(probs_ready, (t + 1) * HEADS)
                link(v.reciprocal(row_inv[:, :], row_sum[:, :]))
                wait_full(v, "pv", t)
                if t == 1:
                    wait_full(v, "oT", 0)
                v.tensor_tensor(o_sb[:, :, :], bank("pv", t)[:, :].rearrange("p (h d) -> p h d", h=HEADS),
                                row_inv[:, :].unsqueeze(2).broadcast_to([P, HEADS, DH]), ALU.mult).then_inc(bank_taken["dve"], 1)
                wait_taken(v, "pv", t)
                v.sem_inc(o_ready, 1)

            select_keys(0)
            softmax_inputs(0)
            select_keys(1)
            wait_taken(v, "gate", 7)
            for c in range(4):
                wait_full(v, "po", c)
                g = gT[:, 2 * c:2 * c + 2, :].rearrange("p c n -> p (c n)")
                v.tensor_tensor(g, g, bank("po", c)[:, :], ALU.mult).then_inc(bank_taken["dve"], 1)
            normalise(0)
            softmax_inputs(1)
            normalise(1)
            for c in range(4):
                wait_full(v, "ao", c)
                g = gT[:, KD + 2 * c:KD + 2 * c + 2, :].rearrange("p c n -> p (c n)")
                v.tensor_tensor(g, g, bank("ao", c)[:, :], ALU.mult).then_inc(bank_taken["dve"], 1)
                wait_taken(v, "ao", c)
                m = gT[:, 2 * c:2 * c + 2, :].rearrange("p c n -> p (c n)")
                v.tensor_tensor(m, m, g, ALU.add).then_inc(merged, 1)
            v.wait_ge(ln_in[1], 32)
            for t in range(TILES):
                for c in range(2):
                    wait_full(v, "mx", t, c)
                    hh = h[:, t, c * 512:(c + 1) * 512]
                    v.scalar_tensor_tensor(hh, hh, ALPHA, bank("mx", t, c)[:, :], ALU.mult, ALU.add).then_inc(bank_taken["dve"], 1)
                    wait_taken(v, "mx", t, c)
                layer_norm(h[:, t, :], [h[:, t, 0:512], h[:, t, 512:1024]], P)

            def topk(u, b):
                n = [0]

                def sig(i):
                    n[0] += 1
                    i.then_inc(topk_step, 1)

                def need(k):
                    v.wait_ge(topk_step, u * TOPK_STEPS + k)
                    v.sem_inc(topk_go, 1)

                v.wait_ge(s_loaded, u + 1)
                v.sem_inc(topk_go, 1)
                S = [s_cur[:, b, c, :] for c in range(2)]
                for c in range(2):
                    sig(v.max(top_v[:, c, 0:8], S[c]))
                for c in range(2):
                    need(1 + c)
                    sig(v.max_index(top_i[:, c, 0:8], top_v[:, c, 0:8], S[c]))
                for c in range(2):
                    sig(v.match_replace(s_left[:, c, :], top_v[:, c, 0:8], S[c], NEG_TAKEN))
                for c in range(2):
                    need(5 + c)
                    sig(v.max(top_v[:, c, 8:16], s_left[:, c, :]))
                for c in range(2):
                    need(7 + c)
                    sig(v.max_index(top_i[:, c, 8:16], top_v[:, c, 8:16], s_left[:, c, :]))
                sig(v.tensor_tensor(cand[:, :, :], top_v[:, 0, :].unsqueeze(2).broadcast_to([P, EK, EK]),
                                    top_v[:, 1, :].unsqueeze(1).broadcast_to([P, EK, EK]), ALU.add))
                flat = cand[:, :, :].rearrange("p a b -> p (a b)")
                need(11)
                sig(v.tensor_copy(top_if[:, :, :], top_i[:, :, :]))
                sig(v.max(best[:, b, 0:8], flat))
                need(13)
                sig(v.max_index(sel[:, 0:8], best[:, b, 0:8], flat))
                sig(v.match_replace(cand2[:, :], best[:, b, 0:8], flat, NEG_TAKEN))
                need(15)
                sig(v.max(best[:, b, 8:16], cand2[:, :]))
                need(16)
                sig(v.max_index(sel[:, 8:16], best[:, b, 8:16], cand2[:, :]))
                v.tensor_scalar(neg_top[:, b:b + 1], best[:, b, 0:1], -1.0, None, ALU.mult).then_inc(top_ready, 1)
                v.wait_ge(topk_step, u * TOPK_STEPS + 17)
                sig(v.tensor_scalar(ab[:, 0, :], sel[:, :], 4, None, ALU.logical_shift_right))
                sig(v.tensor_scalar(ab[:, 1, :], sel[:, :], 15, None, ALU.bitwise_and))
                v.wait_ge(topk_step, u * TOPK_STEPS + 19)
                sig(v.tensor_copy(abf[:, :, :], ab[:, :, :]))
                v.wait_ge(topk_step, u * TOPK_STEPS + 20)
                for c in range(2):
                    sig(v.tensor_tensor(hot[:, c, :, :], abf[:, c, :].unsqueeze(2).broadcast_to([P, EK, EK]),
                                        iota16[:, :].unsqueeze(1).broadcast_to([P, EK, EK]), ALU.is_equal))
                for c in range(2):
                    v.wait_ge(topk_step, u * TOPK_STEPS + 21 + c)
                    sig(v.tensor_tensor(hot[:, c, :, :], hot[:, c, :, :],
                                        top_if[:, c, :].unsqueeze(1).broadcast_to([P, EK, EK]), ALU.mult))
                v.wait_ge(topk_step, u * TOPK_STEPS + 24)
                v.tensor_reduce(pick[:, :, :], hot[:, :, :, :], AX_X, ALU.add).then_inc(ginv_ready, 1)
                v.wait_ge(ginv_ready, u + 1)
                v.scalar_tensor_tensor(expert[:, b, :], pick[:, 0, :], float(NK), pick[:, 1, :], ALU.mult,
                                       ALU.add).then_inc(idx_ready, 1)
                assert n[0] == TOPK_STEPS

            def weights_of(u, b, g):
                v.wait_ge(gelu_ready, u * GPU + g + 1)
                e = slice(g * GRP, (g + 1) * GRP)
                v.tensor_tensor(w_e[:, b, e], act_e[:, b, e], gate[:, b, e], ALU.mult).then_inc(w_ready, 1)

            def unit(u, t, b, nxt):
                v.wait_ge(gexp_ready, u + 1)
                v.reciprocal(ginv[:, b:b + 1], gsum[:, b:b + 1]).then_inc(gate_ready, 1)
                v.wait_ge(gate_ready, 2 * u + 1)
                v.tensor_scalar(gate[:, b, :], gexp[:, b, :], ginv[:, b:b + 1], None, ALU.mult).then_inc(gate_ready, 1)
                v.wait_ge(gate_ready, 2 * u + 2)
                for g in range(GPU):
                    for i in range(GRP):
                        e = g * GRP + i
                        v.wait_ge(landed[e % RING], 16 * (u * (EK // RING) + e // RING + 1))
                        u_row = ring[:, e % RING, 0:D]
                        d = v.tensor_tensor_reduce(u_row, u_row, h[:, t, :], 1.0, 0.0, ALU.mult, ALU.add, dot[:, b, e:e + 1])
                    d.then_inc(dots_ready, 1)
                    if g:
                        weights_of(u, b, g - 1)
                weights_of(u, b, GPU - 1)
                if nxt:
                    topk(u + 2, b)

            for b in range(2):
                topk(b, b)

            def last_norm(t):
                v.wait_ge(ln_in[2], 32)
                v.wait_ge(group_free, AHEAD + (t + 1) * PH * GPU)
                layer_norm(h[:, t, :], [Y[t][0][:, :], Y[t][1][:, :]], P)

            with v.Fori(0, 4) as j:
                for b in range(2):
                    unit(2 * j + b, 0, b, True)
            last_norm(0)
            with v.Fori(4, 7) as j:
                for b in range(2):
                    unit(2 * j + b, 1, b, True)
            for b in range(2):
                unit(UNITS - 2 + b, 1, b, False)
            last_norm(1)


def kernel(**inputs):
    import concourse.bacc as bacc
    from concourse.bass_utils import run_bass_kernel_spmd as run

    a = {k: np.asarray(v) for k, v in inputs.items()}
    nc = bacc.Bacc("TRN2", target_bir_lowering=False, num_devices=1)
    arrays, aps = {}, {}

    def give(name, value):
        value = np.ascontiguousarray(value)
        arrays[name] = value
        aps[name] = nc.dram_tensor(name, value.shape, mybir.dt.from_np(value.dtype), kind="ExternalInput").ap()

    def tables(rot):
        half = rot // 2
        inv = np.float32(10000.0) ** (-np.arange(half, dtype=np.float32) / np.float32(half))
        ang = np.arange(NPOS, dtype=np.float32)[:, None] * inv[None, :].astype(np.float32)
        cos, sin = np.cos(ang), np.sin(ang)
        return np.stack([np.concatenate([cos, cos], 1), np.concatenate([-sin, sin], 1)], 1).astype(np.float32)

    give("x", a["x"][0])
    give("meta", a["meta_tokens"])
    give("ln", np.stack([a["ln0_g"], a["ln0_b"], a["ln1_g"][0], a["ln1_b"][0], a["ln2_g"][0], a["ln2_b"][0]]))
    give("w_in", a["w_in"][0])
    give("b_gate_t", a["b_gate"][0].reshape(2 * KD, P).T)
    give("pool_w", a["pool_w"][0])
    give("pool_scale_t", a["pool_scale"][0].reshape(PG, P).T)
    give("w_pool_up", a["w_pool_up"][0])
    give("w_attn_o", a["w_attn_o"][0])
    give("w_out", a["w_out"][0])
    give("wq", a["peer_wq"][0])
    give("keys_t", a["peer_sub_keys"][0].reshape(2 * PH, NK, P).transpose(2, 0, 1))
    give("uv", np.concatenate([a["peer_u"][0], a["peer_v"][0]], axis=1))
    give("rope_q", tables(DH))
    give("rope_i", tables(32))
    give("ident_in", np.eye(P, dtype=np.float32))
    give("alpha_in", (np.eye(P) * ALPHA).astype(np.float32))
    give("iota_in", np.tile(np.arange(EK, dtype=np.float32), (P, 1)))
    q_pos = N_META + np.arange(SEQ)
    give("causal_in", np.where(np.arange(NPOS)[None, :] <= q_pos[:, None], 0.0, NEG_CAUSAL).astype(np.float32))
    out = nc.dram_tensor("out", (1, SEQ, D), F32, kind="ExternalOutput").ap()
    layer_kernel(nc, *aps.values(), out)
    r = run(nc, [arrays], core_ids=[0])
    return r.results[0]["out"]
```

```python
from contextlib import ExitStack

import concourse.bass as bass
import numpy as np
from concourse import mybir

ALU = mybir.AluOpType
ACT = mybir.ActivationFunctionType
AX_X = mybir.AxisListType.X
F32 = mybir.dt.float32
U32 = mybir.dt.uint32

P = 128
D = 1024
KD = D // P
N_META = 16
SEQ = 256
NPOS = N_META + SEQ
TILES = 2
PW = 512
PG = 4
WINDOWS = (2, 4, 8, 16)
HEADS, DH, KV = 8, 64, 2
IH = 4
QKVI = HEADS * DH + 2 * KV * DH + IH * DH + DH + IH
OFF_K, OFF_V, OFF_QI, OFF_KI, OFF_WI = 512, 640, 768, 1024, 1088
TOPK = 64
SCALE = DH ** -0.5
PH = 8
EK = 16
NK = 128
LN_EPS = 1e-5
ALPHA = 2.0 ** 0.25
NEG_CAUSAL = -3.0e38
NEG_TAKEN = -3.4e38
MASK = 1.0e30
RING = 8
GRP = 2
GPU = EK // GRP
AHEAD = RING // GRP
UNITS = TILES * PH
LOAD_AT = 2
TOPK_STEPS = 24
SLOT = 4096
NK_OF = (N_META + P, NPOS)
POS = (N_META, N_META + P)


def bank_jobs():
    first = [("hT", "M", 0)] + [("hT", "A", c) for c in range(2)]
    first += [(z, t) for z in ("zk", "zs") for t in "AM"] + [("zq", "A")]
    first += [("hT", "B", c) for c in range(2)] + [(z, "B") for z in ("zk", "zs", "zq")]
    first += [("iT", "A"), ("mT",)] + [("is", 0, h) for h in range(IH)]
    first += [("xp", g) for g in range(PG)]
    first += [("qT", 0), ("iT", "B"), ("kT",), ("qT", 1)]
    first += [("gate", c) for c in range(3)]
    first += [("sc", 0, h) for h in range(HEADS)]
    first += [("is", 1, h) for h in range(IH)]
    first += [("gate", c) for c in range(3, 6)]
    first += [("yT", c) for c in range(2)] + [("po", 0, c) for c in range(2)]
    first += [("pm", 0, c) for c in range(2)] + [("pk", 0, c) for c in range(2)] + [("gate", 6), ("pv", 0)]
    first += [("gate", 7), ("oT", 0)] + [("ao", 0, c) for c in range(2)]
    first += [("mx", 0, c) for c in range(2)] + [("h1T", 0, c) for c in range(2)]
    first += [("q2", 0, 0), ("ss", 0, 0), ("q2", 0, 1), ("ss", 0, 1)]
    beside = [("sc", 1, h) for h in range(HEADS)] + [("q2", 0, 2)]
    beside += [("pm", 1, c) for c in range(2)] + [("pk", 1, c) for c in range(2)] + [("ss", 0, 2)]
    beside += [("pk", 1, c) for c in range(2, 4)] + [("pv", 1)] + [("po", 1, c) for c in range(2)]
    beside += [("oT", 1), ("q2", 0, 3)] + [("ao", 1, c) for c in range(2)] + [("ss", 0, 3)]
    beside += [("mx", 1, c) for c in range(2)]
    beside += [("h1T", 1, c) for c in range(2)]
    for c in range(4):
        beside += [("q2", 1, c), ("ss", 1, c)]
    dve = ("is", "sc", "po", "pv", "ao", "mx")
    jobs = [(j, "dve" if j[0] in dve else "act") for j in first + beside]
    at = [n % 8 for n in range(len(first))] + [n % 4 for n in range(len(beside))]
    return jobs, at


JOBS, BANK_AT = bank_jobs()
JOB_AT = {j: n for n, (j, _) in enumerate(JOBS)}


def taken_before(n, who):
    return sum(w == who for _, w in JOBS[:n])


CHUNKS = [("kvqi", 0, ("zk", "B")), ("q", 1, ("zq", "B")), ("xp", 2, ("xp", 3)),
          ("g0", 3, ("gate", 1)), ("g1", 4, ("gate", 3)), ("g2", 5, ("gate", 5)), ("g3", 0, ("gate", 7)),
          ("pool_up", 1, ("po", 0, 1)), ("attn_o", 2, ("ao", 0, 1)),
          ("out0", 3, ("mx", 0, 0)), ("out1", 4, ("mx", 0, 1)),
          ("wq0", 5, ("q2", 0, 0)), ("wq1", 4, ("q2", 0, 1)), ("wq2", 5, ("q2", 0, 2)),
          ("pool_up again", 4, ("po", 1, 1)), ("wq3", 5, ("q2", 0, 3)), ("attn_o again", 4, ("ao", 1, 1)),
          ("out0 again", 5, ("mx", 1, 0)), ("out1 again", 4, ("mx", 1, 1)),
          *((f"wq{c} again", 5 - c % 2, ("q2", 1, c)) for c in range(4))]
SLOT_OF = {c: s for c, s, _ in CHUNKS}


def slot_uses(name):
    n = [c for c, *_ in CHUNKS].index(name)
    return sum(s == SLOT_OF[name] for _, s, _ in CHUNKS[:n + 1])


def layer_kernel(nc, x, meta, ln, w_in, b_gate_t, pool_w, pool_scale_t, w_pool_up, w_attn_o, w_out,
                 wq, keys_t, uv, rope_q, rope_i, ident_in, alpha_in, iota_in, causal_in, out):
    with ExitStack() as ctx:
        def sb(name, shape, dt=F32):
            return ctx.enter_context(nc.sbuf_tensor(name, shape, dt))

        def sem(name):
            return ctx.enter_context(nc.semaphore(name))

        weights = sb("weights", [P, 6 * SLOT])
        ring = weights[:, 0:4 * SLOT].rearrange("p (s n) -> p s n", s=RING)
        h = sb("h", [P, TILES, D])
        h_meta = weights[0:N_META, 5 * SLOT:5 * SLOT + D]
        hT = sb("hT", [P, KD, NPOS])
        h1T = hT[:, :, :].rearrange("p k n -> p (k n)")[:, 0:TILES * D].rearrange("p (t k n) -> p t k n", t=TILES, k=KD)
        ln_g = sb("ln_g", [P, D])
        ln_b = sb("ln_b", [P, D])
        gT = sb("gT", [P, TILES, 2 * KD, P])
        q2T = gT
        arena = sb("arena", [P, 10368])
        z = arena[:, 0:2184].rearrange("p (t n) -> p t n", t=TILES)
        z_m = arena[:, 2184:2508]
        r_qk = arena[:, 2508:3788].rearrange("p (t h d) -> p t h d", t=TILES, d=DH)
        r_k = arena[:, 3788:4556].rearrange("p (t g c d) -> p t g c d", t=3, g=KV, c=2)
        r_i = arena[:, 4556:5708].rearrange("p (t h d) -> p t h d", t=3, d=DH)
        r_mk = arena[:, 5708:5836].rearrange("p (h d) -> p h d", d=DH)
        tmp = arena[:, 5836:6476]
        tabs_q = arena[:, 6476:6860].rearrange("p (t c d) -> p t c d", t=3, c=2)
        tabs_i = arena[:, 6860:7052].rearrange("p (t c d) -> p t c d", t=3, c=2)
        xpT = arena[:, 7052:8140].rearrange("p (g n) -> p g n", g=PG)
        wsum = arena[:, 8140:8684].rearrange("p (c n) -> p c n", c=2)
        pw = arena[:, 8684:9196].rearrange("p (g n) -> p g n", g=PG)
        w_small = arena[:, 9196:9740].rearrange("p (k n) -> p k n", k=KD)
        probs = arena[:, 0:2176].rearrange("p (h n) -> p h n", h=HEADS)
        o_sb = arena[:, 0:HEADS * DH].rearrange("p (h d) -> p h d", h=HEADS)
        pT_meta = arena[:, 2176:3200].rearrange("p (h n) -> p h n", h=HEADS)
        pT = arena[:, 3200:5248].rearrange("p (h c n) -> p h c n", h=HEADS, c=2)
        s_all = arena[:, 5248:7296].rearrange("p (u n) -> p u n", u=PH)
        diag = arena[:, 7296:8320].rearrange("p (s n) -> p s n", s=RING)
        keysT = arena[:, 8320:10368].rearrange("p (c n) -> p c n", c=2 * PH)
        wi = sb("wi", [P, TILES, IH])
        v_sb = sb("v_sb", [P, 3, KV * DH])
        iT = sb("iT", [P, TILES, 2, P])
        kiT = sb("kiT", [P, NPOS])
        qT = sb("qT", [P, TILES, 4, P])
        kT = sb("kT", [P, KV, NPOS])
        rel = sb("rel", [P, NPOS])
        isum = sb("isum", [P, 2, NPOS])
        causal = sb("causal", [P, TILES, NPOS])
        m8 = sb("m8", [P, 8])
        neg_max = sb("neg_max", [P, HEADS])
        row_sum = sb("row_sum", [P, HEADS])
        row_inv = sb("row_inv", [P, HEADS])
        oT = sb("oT", [P, TILES, 4, P])
        yT = oT
        ident = sb("ident", [P, P])
        alpha_i = sb("alpha_i", [P, P])
        iota16 = sb("iota16", [P, EK])
        bg = sb("bg", [P, 2 * KD])
        ps = sb("ps", [P, PG])
        stats = sb("stats", [P, 2, 6])
        mv = sb("mv", [P, 2])
        nrm = sb("nrm", [P, 8])
        s_cur = sb("s_cur", [P, 2, 2, NK])
        s_left = sb("s_left", [P, 2, NK])
        top_v = sb("top_v", [P, 2, EK])
        top_i = sb("top_i", [P, 2, EK], U32)
        top_if = sb("top_if", [P, 2, EK])
        cand = sb("cand", [P, EK, EK])
        cand2 = sb("cand2", [P, EK * EK])
        best = sb("best", [P, 2, EK])
        sel = sb("sel", [P, EK], U32)
        ab = sb("ab", [P, 2, EK], U32)
        abf = sb("abf", [P, 2, EK])
        hot = sb("hot", [P, 2, EK, EK])
        pick = sb("pick", [P, 2, EK])
        expert = sb("expert", [P, 2, EK], U32)
        neg_top = sb("neg_top", [P, 2])
        gexp = sb("gexp", [P, 2, EK])
        gsum = sb("gsum", [P, 2])
        ginv = sb("ginv", [P, 2])
        gate = sb("gate", [P, 2, EK])
        dot = sb("dot", [P, 2, EK])
        act_e = sb("act_e", [P, 2, EK])
        w_e = sb("w_e", [P, 2, EK])

        banks = [ctx.enter_context(nc.psum_tensor(f"bank{n}", [P, 512], F32)) for n in range(8)]
        Y = [(banks[4], banks[5]), (banks[6], banks[7])]

        x_in = [sem(f"x_in_{t}") for t in "ABM"]
        ln_in = [sem(f"ln{n}_in") for n in range(3)]
        const_in = sem("const_in")
        ident_sem = sem("ident_in")
        small_in = sem("small_in")
        keys_in = sem("keys_in")
        slot_in = [sem(f"slot_in{s}") for s in range(6)]
        bank_full = sem("bank_full")
        bank_taken = {"act": sem("bank_taken_act"), "dve": sem("bank_taken_dve")}
        dve_step = sem("dve_step")
        pool_step = sem("pool_step")
        var_ready = sem("var_ready")
        std_ready = sem("std_ready")
        ln_done = sem("ln_done")
        rotated = sem("rotated")
        scored = sem("scored")
        probs_ready = sem("probs_ready")
        o_ready = sem("o_ready")
        merged = sem("merged")
        windows_done = sem("windows_done")
        s_loaded = sem("s_loaded")
        topk_step = sem("topk_step")
        topk_go = sem("topk_go")
        idx_ready = sem("idx_ready")
        top_ready = sem("top_ready")
        gexp_ready = sem("gexp_ready")
        ginv_ready = sem("ginv_ready")
        gate_ready = sem("gate_ready")
        landed = [sem(f"landed{s}") for s in range(RING)]
        gather_go = sem("gather_go")
        act_go = sem("act_go")
        dots_ready = sem("dots_ready")
        gelu_ready = sem("gelu_ready")
        w_ready = sem("w_ready")
        diag_ready = sem("diag_ready")
        group_free = sem("group_free")
        y_ready = sem("y_ready")
        out_done = sem("out_done")

        def bank(*job):
            return banks[BANK_AT[JOB_AT[job]]]

        def wait_free(pe, *job):
            n = JOB_AT[job]
            older = [m for m in range(n) if BANK_AT[m] == BANK_AT[n]]
            if older:
                wait_taken(pe, *JOBS[older[-1]][0])

        def wait_full(eng, *job):
            eng.wait_ge(bank_full, JOB_AT[job] + 1)

        def wait_taken(eng, *job):
            n = JOB_AT[job]
            who = JOBS[n][1]
            eng.wait_ge(bank_taken[who], taken_before(n, who) + 1)

        def chunk(name, k):
            s = SLOT_OF[name]
            return weights[:, s * SLOT:(s + 1) * SLOT].rearrange("p (k n) -> p k n", k=k)

        def wait_chunk(pe, name):
            pe.wait_ge(slot_in[SLOT_OF[name]], 16 * slot_uses(name))

        rows = {"A": (0, P), "B": (1, P), "M": (2, N_META)}
        where = {"M": 0, "A": POS[0], "B": POS[1]}
        w_in_k = w_in.rearrange("(k p) n -> p k n", p=P)
        SRC = {
            "kvqi": w_in_k[:, :, PW + OFF_K:PW + OFF_K + 512], "q": w_in_k[:, :, PW:PW + 512],
            "xp": w_in_k[:, :, 0:PW],
            **{f"g{c}": w_in_k[:, :, PW + QKVI + 512 * c:PW + QKVI + 512 * c + 512] for c in range(4)},
            "pool_up": w_pool_up.rearrange("(k p) n -> p k n", p=P),
            "attn_o": w_attn_o.rearrange("(k p) n -> p k n", p=P),
            **{f"out{c}": w_out.rearrange("(k p) n -> p k n", p=P)[:, :, 512 * c:512 * c + 512] for c in range(2)},
            **{f"wq{c}": wq.rearrange("(k p) n -> p k n", p=P)[:, :, 512 * c:512 * c + 512] for c in range(4)},
        }
        SRC.update({f"{name} again": src for name, src in SRC.items()})

        block = ctx.enter_context(nc.Block())

        @block.sync
        def _(sp):
            def load_ln(n):
                sp.dma_start(ln_g[:, :], ln[2 * n:2 * n + 1, :].partition_broadcast(P)).then_inc(ln_in[n], 16)
                sp.dma_start(ln_b[:, :], ln[2 * n + 1:2 * n + 2, :].partition_broadcast(P)).then_inc(ln_in[n], 16)

            def load_chunk(n):
                name, s, _ = CHUNKS[n]
                if name == "g2":
                    wait_full(sp, "hT", "M", 0)
                older = [last for _, t, last in CHUNKS[:n] if t == s]
                if older:
                    wait_full(sp, *older[-1])
                k = SRC[name].shape[1]
                sp.dma_start(chunk(name, k), SRC[name]).then_inc(slot_in[s], 16)

            sp.dma_start(h_meta, meta).then_inc(x_in[2], 16)
            sp.dma_start(h[:, 0, :], x[0:P, :]).then_inc(x_in[0], 16)
            load_ln(0)
            sp.dma_start(ident[:, :], ident_in).then_inc(ident_sem, 16)
            load_chunk(0)
            sp.dma_start(w_small, w_in_k[:, :, PW + OFF_KI:PW + QKVI]).then_inc(small_in, 16)
            sp.dma_start(h[:, 1, :], x[P:SEQ, :]).then_inc(x_in[1], 16)
            for t, (n, rows_) in rows.items():
                r = where[t]
                sp.dma_start(tabs_q[0:rows_, n, :, :], rope_q[r:r + rows_]).then_inc(const_in, 16)
                sp.dma_start(tabs_i[0:rows_, n, :, :], rope_i[r:r + rows_]).then_inc(const_in, 16)
            load_chunk(1)
            load_chunk(2)
            sp.dma_start(causal[:, :, :], causal_in.rearrange("(t p) n -> p t n", p=P)).then_inc(const_in, 16)
            sp.dma_start(bg[:, :], b_gate_t).then_inc(const_in, 16)
            sp.dma_start(ps[:, :], pool_scale_t).then_inc(const_in, 16)
            sp.dma_start(iota16[:, :], iota_in).then_inc(const_in, 16)
            sp.dma_start(alpha_i[:, :], alpha_in).then_inc(const_in, 16)
            sp.dma_start(pw[:, :, :], pool_w.rearrange("g c d -> c g d")).then_inc(const_in, 16)
            for n in range(3, 6):
                load_chunk(n)
            sp.wait_ge(ln_done, 3)
            load_ln(1)
            for n in range(6, len(CHUNKS)):
                if CHUNKS[n][0] == "out0":
                    wait_full(sp, "yT", 1)
                    sp.dma_start(keysT[:, :, :], keys_t).then_inc(keys_in, 16)
                if CHUNKS[n][0] == "wq0 again":
                    sp.wait_ge(ln_done, 5)
                    load_ln(2)
                load_chunk(n)
            for t in range(TILES):
                sp.wait_ge(ln_done, 6 + t)
                sp.dma_start(out[0, t * P:(t + 1) * P, :], h[:, t, :]).then_inc(out_done, 16)
            sp.wait_ge(out_done, 16 * TILES)

        N_CONST = 12

        @block.gpsimd
        def _(pool):
            steps = 0
            for g, w in enumerate(WINDOWS):
                wait_taken(pool, "xp", g)
                src, width, first = xpT[:, g, :], 1, 0
                n = 0
                while width < w:
                    first += width
                    dst = wsum[:, n % 2, :]
                    pool.tensor_tensor(dst[:, first:NPOS], src[:, first:NPOS], src[:, first - width:NPOS - width],
                                       ALU.add).then_inc(pool_step, 1)
                    steps += 1
                    pool.wait_ge(pool_step, steps)
                    src, width, n = dst, 2 * width, n + 1
                pool.tensor_scalar(src[:, N_META:NPOS], src[:, N_META:NPOS], 1.0 / w, None, ALU.mult).then_inc(pool_step, 1)
                steps += 1
                pool.wait_ge(pool_step, steps)
                pool.tensor_tensor(xpT[:, g, N_META:NPOS], src[:, N_META:NPOS], xpT[:, g, N_META:NPOS],
                                   ALU.subtract).then_inc(windows_done, 1)
                pool.wait_ge(windows_done, g + 1)

            wait_full(pool, "mx", 0, 1)

            def gather_unit(u, b):
                pool.wait_ge(idx_ready, u + 1)
                for e in range(EK):
                    if e % GRP == 0:
                        pool.wait_ge(group_free, u * GPU + e // GRP + 1)
                        pool.sem_inc(gather_go, 1)
                    pool.indirect_dma_start(ring[:, e % RING, :], None, uv,
                                            bass.IndirectOffsetOnAxis(ap=expert[:, b, e:e + 1], axis=0)
                                            ).then_inc(landed[e % RING], 16)

            with pool.Fori(0, UNITS // 2) as j:
                for b in range(2):
                    gather_unit(2 * j + b, b)

        @block.scalar
        def _(act):
            def take(dst, src, last=True, **kw):
                i = act.activation(dst, src, kw.pop("func", ACT.Copy), **kw)
                if last:
                    i.then_inc(bank_taken["act"], 1)
                return i

            def std(n):
                act.wait_ge(var_ready, n)
                act.activation(nrm[:, 1:2], nrm[:, 0:1], ACT.Sqrt).then_inc(std_ready, 1)

            def take_h(t):
                n, r = rows[t]
                for c in range(1 if t == "M" else 2):
                    wait_full(act, "hT", t, c)
                    kk = KD if t == "M" else 4
                    take(hT[:, c * 4:c * 4 + kk, where[t]:where[t] + r],
                         bank("hT", t, c)[:, 0:kk * r].rearrange("p (k n) -> p k n", k=kk))

            def take_z(kind, t):
                n, r = rows[t]
                wait_full(act, kind, t)
                src = bank(kind, t)
                if kind == "zk":
                    take(v_sb[0:r, n, :], src[0:r, 128:256], last=False)
                    if t == "M":
                        take(z_m[0:r, 0:256], src[0:r, 0:256])
                    else:
                        take(z[:, n, OFF_K:OFF_K + 512], src[:, :])
                elif kind == "zq":
                    take(z[:, n, 0:512], src[:, :])
                elif t == "M":
                    take(z_m[0:r, 256:320], src[0:r, 0:64])
                else:
                    take(wi[:, n, :], src[:, 64:68], last=False, scale=IH ** -0.5 * DH ** -0.5)
                    take(z[:, n, OFF_KI:QKVI], src[:, 0:68])

            def take_index(t):
                n, _ = rows[t]
                wait_full(act, "iT", t)
                src = bank("iT", t)
                take(iT[:, n, :, :], src[:, 0:2 * P].rearrange("p (c n) -> p c n", c=2), last=False)
                take(kiT[:, where[t]:where[t] + P], src[:, 2 * P:3 * P])

            def take_queries(t):
                wait_full(act, "qT", t)
                take(qT[:, t, :, :], bank("qT", t)[:, :].rearrange("p (c n) -> p c n", c=4))

            def take_gates(c):
                wait_full(act, "gate", c)
                for i in range(2):
                    take(gT[:, :, 2 * c + i, :], bank("gate", c)[:, i * SEQ:(i + 1) * SEQ].rearrange("p (t n) -> p t n", t=TILES),
                         func=ACT.Sigmoid, bias=bg[:, 2 * c + i:2 * c + i + 1], last=(i == 1))

            def exp_scores(t):
                for hd in range(HEADS):
                    act.wait_ge(scored, t * HEADS + hd + 1)
                    act.activation(probs[:, hd, 0:NK_OF[t]], probs[:, hd, 0:NK_OF[t]], ACT.Exp,
                                   bias=neg_max[:, hd:hd + 1], scale=-1.0,
                                   accum_out=row_sum[:, hd:hd + 1]).then_inc(probs_ready, 1)

            def take_meta_probs(t, c):
                wait_full(act, "pm", t, c)
                take(pT_meta[0:N_META, 4 * c:4 * c + 4, :],
                     bank("pm", t, c)[0:N_META, :].rearrange("p (h n) -> p h n", h=4))

            def take_probs(t, c):
                wait_full(act, "pk", t, c)
                if t == 0:
                    take(pT[:, 4 * c:4 * c + 4, 0, :], bank("pk", t, c)[:, :].rearrange("p (h n) -> p h n", h=4))
                else:
                    take(pT[:, 2 * c:2 * c + 2, :, :],
                         bank("pk", t, c)[:, :].rearrange("p (h c n) -> p h c n", h=2, c=2))

            def take_block(name, t, c, dst):
                wait_full(act, name, t, c)
                take(dst[:, t, 4 * c:4 * c + 4, :], bank(name, t, c)[:, :].rearrange("p (k n) -> p k n", k=4))

            def take_o(t):
                wait_full(act, "oT", t)
                take(oT[:, t, :, :], bank("oT", t)[:, :].rearrange("p (c n) -> p c n", c=4))

            def take_ss(t, c):
                wait_full(act, "ss", t, c)
                if t:
                    act.wait_ge(s_loaded, PH)
                take(s_all[:, 2 * c:2 * c + 2, :], bank("ss", t, c)[:, :].rearrange("p (u n) -> p u n", u=2))

            std(1)
            take_h("M")
            std(2)
            take_h("A")
            std(3)
            for kind in ("zk", "zs"):
                for t in "AM":
                    take_z(kind, t)
            take_z("zq", "A")
            take_h("B")
            for kind in ("zk", "zs", "zq"):
                take_z(kind, "B")
            take_index("A")
            wait_full(act, "mT")
            src = bank("mT")
            take(kiT[:, 0:N_META], src[:, 0:N_META], last=False)
            take(kT[:, :, 0:N_META], src[:, N_META:3 * N_META].rearrange("p (g n) -> p g n", g=KV))
            for g in range(PG):
                wait_full(act, "xp", g)
                take(xpT[:, g, :], bank("xp", g)[:, 0:NPOS])
            take_queries(0)
            take_index("B")
            wait_full(act, "kT")
            for t in range(TILES):
                take(kT[:, :, POS[t]:POS[t] + P],
                     bank("kT")[:, t * 256:t * 256 + 256].rearrange("p (g n) -> p g n", g=KV), last=(t == 1))
            take_queries(1)
            act.wait_ge(const_in, 16 * N_CONST)
            for c in range(3):
                take_gates(c)
            exp_scores(0)
            for c in range(3, 6):
                take_gates(c)
            for c in range(2):
                wait_full(act, "yT", c)
                for i in range(2):
                    g = 2 * c + i
                    take(yT[:, :, g, :], bank("yT", c)[:, i * SEQ:(i + 1) * SEQ].rearrange("p (t n) -> p t n", t=TILES),
                         scale=ps[:, g:g + 1], last=(i == 1))
            for c in range(2):
                take_meta_probs(0, c)
            for c in range(2):
                take_probs(0, c)
            take_gates(6)
            take_gates(7)
            take_o(0)
            std(4)
            for c in range(2):
                take_block("h1T", 0, c, h1T)

            def exp_gates(u, b):
                act.wait_ge(top_ready, u + 1)
                act.activation(gexp[:, b, :], best[:, b, :], ACT.Exp, bias=neg_top[:, b:b + 1],
                               accum_out=gsum[:, b:b + 1]).then_inc(gexp_ready, 1)

            def load_scores(u, b):
                act.activation(s_cur[:, b, :, :].rearrange("p c n -> p (c n)"), s_all[:, u, :],
                               ACT.Copy).then_inc(s_loaded, 1)

            take_block("q2", 0, 0, q2T)
            take_ss(0, 0)
            wait_taken(act, "ss", 0, 0)
            for b in range(2):
                load_scores(b, b)
            take_block("q2", 0, 1, q2T)
            take_ss(0, 1)
            for b in range(2):
                exp_gates(b, b)

            def beside(n):
                if n == 6:
                    exp_scores(1)
                if n == 9:
                    take_block("q2", 0, 2, q2T)
                if n == 10:
                    take_meta_probs(1, 0)
                    take_meta_probs(1, 1)
                if n == 11:
                    take_probs(1, 0)
                    take_probs(1, 1)
                if n == 12:
                    take_ss(0, 2)
                if n == 14:
                    take_probs(1, 2)
                    take_probs(1, 3)
                if n == 21:
                    take_o(1)
                if n == 23:
                    take_block("q2", 0, 3, q2T)
                if n == 27:
                    take_ss(0, 3)
                if n == 36:
                    std(5)
                if n == 43:
                    for c in range(2):
                        take_block("h1T", 1, c, h1T)
                if n in (47, 52, 57, 61):
                    take_block("q2", 1, (47, 52, 57, 61).index(n), q2T)
                if n in (50, 55, 60, 63):
                    take_ss(1, (50, 55, 60, 63).index(n))

            def diagonals(u, b, g):
                act.wait_ge(group_free, u * GPU + g + 1)
                act.wait_ge(w_ready, u * GPU + g + 1)
                for i in range(GRP):
                    e = g * GRP + i
                    d = act.activation(diag[:, e % RING, :], ident[:, :], ACT.Copy, scale=w_e[:, b, e:e + 1])
                d.then_inc(diag_ready, 1)

            def unit(u, b, score_row):
                for g in range(GPU):
                    act.wait_ge(dots_ready, u * GPU + g + 1)
                    act.activation(act_e[:, b, g * GRP:(g + 1) * GRP], dot[:, b, g * GRP:(g + 1) * GRP],
                                   ACT.Gelu).then_inc(gelu_ready, 1)
                    if g:
                        diagonals(u, b, g - 1)
                    if g == GPU - 1:
                        diagonals(u, b, g)
                    if isinstance(u, int) and u < PH:
                        beside(u * GPU + g)
                    if g == LOAD_AT and score_row is not None:
                        act.wait_ge(top_ready, u + 1)
                        if isinstance(u, int):
                            wait_taken(act, "ss", (u + 2) // PH, (u + 2) % PH // 2)
                        else:
                            act.sem_inc(act_go, 1)
                        load_scores(score_row, b)

            for u in range(PH):
                unit(u, u % 2, (u + 2) % PH)
                exp_gates(u + 2, u % 2)
            std(6)
            wait_taken(act, "ss", 1, 3)
            with act.Fori(4, 7) as j:
                for b in range(2):
                    u = 2 * j + b
                    unit(u, b, u + 2 - PH)
                    exp_gates(u + 2, b)
            for b in range(2):
                unit(UNITS - 2 + b, b, None)
            std(7)

        @block.tensor
        def _(pe):
            def full(mm):
                mm.then_inc(bank_full, 1)

            def stream_t(t):
                n, r = rows[t]
                src = h_meta if t == "M" else h[:, n, :]
                pe.wait_ge(ln_done, "MAB".index(t) + 1)
                for c in range(1 if t == "M" else 2):
                    wait_free(pe, "hT", t, c)
                    kk = KD if t == "M" else 4
                    for k in range(kk):
                        mm = pe.transpose(bank("hT", t, c)[:, k * r:(k + 1) * r],
                                          src[:, (4 * c + k) * P:(4 * c + k + 1) * P], ident[0:r, 0:r])
                    full(mm)

            def project(job, t, w, cols):
                n, r = rows[t]
                wait_free(pe, *job)
                for k in range(KD):
                    mm = pe.matmul(bank(*job)[0:r, 0:cols], hT[:, k, where[t]:where[t] + r], w[:, k, 0:cols],
                                   start=(k == 0), stop=(k == KD - 1))
                full(mm)

            def project_z(kind, t):
                cols = {"zk": 256 if t == "M" else 512, "zs": 64 if t == "M" else 68, "zq": 512}[kind]
                w = {"zk": chunk("kvqi", KD), "zs": w_small, "zq": chunk("q", KD)}[kind]
                project((kind, t), t, w, cols)

            pe.wait_ge(ident_sem, 16)
            stream_t("M")
            stream_t("A")
            wait_taken(pe, "hT", "A", 1)
            wait_chunk(pe, "kvqi")
            for t in "AM":
                project_z("zk", t)
            pe.wait_ge(small_in, 16)
            for t in "AM":
                project_z("zs", t)
            wait_chunk(pe, "q")
            project_z("zq", "A")
            stream_t("B")
            wait_taken(pe, "hT", "B", 1)
            for kind in ("zk", "zs", "zq"):
                project_z(kind, "B")

            def pool_inputs():
                wait_chunk(pe, "xp")
                for g in range(PG):
                    wait_free(pe, "xp", g)
                    for k in range(KD):
                        mm = pe.matmul(bank("xp", g)[:, 0:NPOS], chunk("xp", KD)[:, k, g * P:(g + 1) * P], hT[:, k, :],
                                       start=(k == 0), stop=(k == KD - 1))
                    full(mm)

            def transposes(job, srcs, r=P):
                wait_free(pe, *job)
                for i, s in enumerate(srcs):
                    mm = pe.transpose(bank(*job)[:, i * r:(i + 1) * r], s, ident[0:r, 0:r])
                full(mm)

            def transpose_index(t):
                transposes(("iT", t), [r_i[:, rows[t][0], 2 * c:2 * c + 2, :].rearrange("p h d -> p (h d)") for c in range(3)])

            def transpose_queries(t):
                transposes(("qT", t), [r_qk[:, t, 2 * c:2 * c + 2, :].rearrange("p h d -> p (h d)") for c in range(4)])

            pe.wait_ge(rotated, 1)
            transpose_index("A")
            pe.wait_ge(rotated, 2)
            M = N_META
            transposes(("mT",), [r_i[0:M, 2, 4:6, :].rearrange("p h d -> p (h d)")]
                       + [r_k[0:M, 2, g, :, :].rearrange("p c d -> p (c d)") for g in range(KV)], M)

            def index_scores(t):
                for hd in range(IH):
                    half = slice(64 * (hd % 2), 64 * (hd % 2) + 64)
                    wait_free(pe, "is", t, hd)
                    if hd == 0 and t == 0:
                        wait_taken(pe, "mT")
                    full(pe.matmul(bank("is", t, hd)[:, 0:NK_OF[t]], iT[half, t, hd // 2, :],
                                   kiT[half, 0:NK_OF[t]], start=True, stop=True))

            index_scores(0)
            pool_inputs()
            pe.wait_ge(rotated, 3)
            transpose_queries(0)
            pe.wait_ge(rotated, 4)
            transpose_index("B")
            pe.wait_ge(rotated, 5)
            transposes(("kT",), [r_k[:, t, g, :, :].rearrange("p c d -> p (c d)") for t in range(TILES) for g in range(KV)])
            transpose_queries(1)

            def gates(c):
                name = f"g{c // 2}"
                wait_chunk(pe, name)
                wait_free(pe, "gate", c)
                for i in range(2):
                    col = (2 * (c % 2) + i) * P
                    for k in range(KD):
                        mm = pe.matmul(bank("gate", c)[:, i * SEQ:(i + 1) * SEQ], chunk(name, KD)[:, k, col:col + P],
                                       hT[:, k, N_META:NPOS], start=(k == 0), stop=(k == KD - 1))
                full(mm)

            for c in range(3):
                gates(c)

            def attention_score(t, hd):
                half = slice(64 * (hd % 2), 64 * (hd % 2) + 64)
                wait_free(pe, "sc", t, hd)
                if hd == 0 and t == 0:
                    wait_taken(pe, "qT", 1)
                full(pe.matmul(bank("sc", t, hd)[:, 0:NK_OF[t]], qT[half, t, hd // 2, :],
                               kT[half, hd // 4, 0:NK_OF[t]], start=True, stop=True))

            def transpose_meta_probs(t, c):
                pe.wait_ge(probs_ready, t * HEADS + 4 * c + 4)
                wait_free(pe, "pm", t, c)
                for i in range(4):
                    mm = pe.transpose(bank("pm", t, c)[0:N_META, i * P:(i + 1) * P],
                                      probs[:, 4 * c + i, 0:N_META], ident[:, :])
                full(mm)

            def transpose_probs(t, c):
                per = 4 // (t + 1)
                wait_free(pe, "pk", t, c)
                for i in range(per):
                    for b in range(t + 1):
                        mm = pe.transpose(bank("pk", t, c)[:, (i * (t + 1) + b) * P:(i * (t + 1) + b + 1) * P],
                                          probs[:, c * per + i, POS[b]:POS[b] + P], ident[:, :])
                full(mm)

            def attend(t):
                wait_free(pe, "pv", t)
                wait_taken(pe, "pk", t, 2 * (t + 1) - 1)
                for hd in range(HEADS):
                    g = slice(64 * (hd // 4), 64 * (hd // 4) + 64)
                    o = bank("pv", t)[:, hd * DH:(hd + 1) * DH]
                    pe.matmul(o, pT_meta[0:N_META, hd, :], v_sb[0:N_META, 2, g], start=True, stop=False)
                    for b in range(t + 1):
                        mm = pe.matmul(o, pT[:, hd, b, :], v_sb[:, b, g], start=False, stop=(b == t))
                full(mm)

            def transpose_o(t):
                pe.wait_ge(o_ready, t + 1)
                transposes(("oT", t), [o_sb[:, 2 * c:2 * c + 2, :].rearrange("p h d -> p (h d)") for c in range(4)])

            def blocks(name, w, src, t, c, tiles, again=""):
                kk = src.shape[1]
                if tiles[0] == 0:
                    wait_chunk(pe, w + again)
                    wait_free(pe, name, t, c)
                for i in tiles:
                    col = (i if name == "q2" else 4 * c + i) * P
                    for k in range(kk):
                        mm = pe.matmul(bank(name, t, c)[:, i * P:(i + 1) * P], chunk(w + again, kk)[:, k, col:col + P],
                                       src[:, k, :], start=(k == 0), stop=(k == kk - 1))
                if tiles[-1] == 3:
                    full(mm)

            def output_products(t, products, again=""):
                for m in products:
                    c, k = m // KD, m % KD
                    if k == 0:
                        wait_chunk(pe, f"out{c}" + again)
                        pe.wait_ge(merged, 2 * t + 2)
                        wait_free(pe, "mx", t, c)
                    mm = pe.matmul(bank("mx", t, c)[:, :], gT[:, t, k, :], chunk(f"out{c}" + again, KD)[:, k, :],
                                   start=(k == 0), stop=(k == KD - 1))
                    if k == KD - 1:
                        full(mm)

            def transpose_h1(t):
                pe.wait_ge(ln_done, 4 + t)
                for c in range(2):
                    transposes(("h1T", t, c), [h[:, t, (4 * c + k) * P:(4 * c + k + 1) * P] for k in range(4)])

            def queries(t, c, tiles, again=""):
                if c == 0 and tiles[0] == 0:
                    wait_taken(pe, "h1T", t, 1)
                blocks("q2", f"wq{c}", h1T[:, t, :, :], t, c, tiles, again)

            def key_scores(t, c):
                wait_free(pe, "ss", t, c)
                wait_taken(pe, "q2", t, c)
                for i in range(4):
                    n = 4 * c + i
                    mm = pe.matmul(bank("ss", t, c)[:, i * NK:(i + 1) * NK], q2T[:, t, n, :], keysT[:, n, :],
                                   start=True, stop=True)
                full(mm)

            for hd in range(HEADS):
                attention_score(0, hd)
            index_scores(1)
            for c in range(3, 6):
                gates(c)
            pe.wait_ge(windows_done, PG)
            for c in range(2):
                wait_free(pe, "yT", c)
                for i in range(2):
                    g = 2 * c + i
                    mm = pe.matmul(bank("yT", c)[:, i * SEQ:(i + 1) * SEQ], pw[:, g, :], xpT[:, g, N_META:NPOS],
                                   start=True, stop=True)
                full(mm)
            wait_taken(pe, "yT", 1)
            for c in range(2):
                blocks("po", "pool_up", yT[:, 0, :, :], 0, c, range(4))
            for c in range(2):
                transpose_meta_probs(0, c)
            for c in range(2):
                transpose_probs(0, c)
            gates(6)
            attend(0)
            gates(7)
            transpose_o(0)
            wait_taken(pe, "oT", 0)
            for c in range(2):
                blocks("ao", "attn_o", oT[:, 0, :, :], 0, c, range(4))
            output_products(0, range(2 * KD))
            pe.sem_inc(group_free, AHEAD)
            transpose_h1(0)
            pe.wait_ge(keys_in, 16)
            for c in range(2):
                queries(0, c, range(4))
                key_scores(0, c)

            def start_sum(t):
                for c in range(2):
                    if t == 0:
                        for b in range(4, 8):
                            last = [m for m in range(len(JOBS)) if BANK_AT[m] == b][-1]
                            wait_taken(pe, *JOBS[last][0])
                    pe.matmul(Y[t][c][:, :], alpha_i[:, :], h[:, t, c * 512:(c + 1) * 512], start=True, stop=False,
                              skip_group_check=True)

            def beside(n):
                first, second = range(0, 2), range(2, 4)
                if n < 4:
                    attention_score(1, 2 * n)
                    attention_score(1, 2 * n + 1)
                elif n < 8:
                    queries(0, 2, [n - 4])
                elif n == 8:
                    transpose_meta_probs(1, 0)
                    transpose_meta_probs(1, 1)
                elif n == 9:
                    transpose_probs(1, 0)
                    transpose_probs(1, 1)
                elif n == 10:
                    key_scores(0, 2)
                elif n == 12:
                    transpose_probs(1, 2)
                    transpose_probs(1, 3)
                elif n == 15:
                    attend(1)
                    blocks("po", "pool_up", yT[:, 1, :, :], 1, 0, first, " again")
                elif n == 16:
                    blocks("po", "pool_up", yT[:, 1, :, :], 1, 0, second, " again")
                elif n == 17:
                    blocks("po", "pool_up", yT[:, 1, :, :], 1, 1, first, " again")
                elif n == 18:
                    blocks("po", "pool_up", yT[:, 1, :, :], 1, 1, second, " again")
                elif n == 19:
                    transpose_o(1)
                elif n in (20, 21):
                    queries(0, 3, first if n == 20 else second)
                elif n == 22:
                    wait_taken(pe, "oT", 1)
                    blocks("ao", "attn_o", oT[:, 1, :, :], 1, 0, first, " again")
                elif n == 23:
                    blocks("ao", "attn_o", oT[:, 1, :, :], 1, 0, second, " again")
                elif n == 24:
                    blocks("ao", "attn_o", oT[:, 1, :, :], 1, 1, first, " again")
                elif n == 25:
                    blocks("ao", "attn_o", oT[:, 1, :, :], 1, 1, second, " again")
                    key_scores(0, 3)
                elif 28 <= n < 34:
                    output_products(1, range(3 * (n - 28), min(3 * (n - 27), 2 * KD)), " again")
                elif n == 41:
                    transpose_h1(1)
                elif n in (44, 49, 53, 58):
                    if n > 49:
                        key_scores(1, (44, 49, 53, 58).index(n) - 1)
                    queries(1, (44, 49, 53, 58).index(n), first, " again")
                elif n in (45, 50, 54, 59):
                    queries(1, (45, 50, 54, 59).index(n), second, " again")
                elif n == 48:
                    key_scores(1, 0)
                elif n == 62:
                    key_scores(1, 3)

            def unit(u, t, final):
                for g in range(GPU):
                    pe.wait_ge(diag_ready, u * GPU + g + 1)
                    for i in range(GRP):
                        s = (g * GRP + i) % RING
                        for c in range(2):
                            last = final and g == GPU - 1 and i == GRP - 1
                            mm = pe.matmul(Y[t][c][:, :], diag[:, s, :], ring[:, s, D + c * 512:D + (c + 1) * 512],
                                           start=False, stop=last, skip_group_check=True)
                    mm.then_inc(group_free, 1)
                    if isinstance(u, int):
                        beside(u * GPU + g)

            start_sum(0)
            for u in range(PH):
                unit(u, 0, u == PH - 1)
            start_sum(1)
            with pe.Fori(4, 8) as j:
                for b in range(2):
                    unit(2 * j + b, 1, False)

        @block.vector
        def _(v):
            count = [0, 0]

            def link(i):
                count[0] += 1
                i.then_inc(dve_step, 1)
                v.wait_ge(dve_step, count[0])

            def step(i):
                count[0] += 1
                i.then_inc(dve_step, 1)

            def sync():
                v.wait_ge(dve_step, count[0])

            def norm_begin(dst, halves, r):
                for c in range(2):
                    step(v.bn_stats(stats[0:r, c, :], halves[c]))
                sync()
                link(v.bn_aggr(mv[0:r, :], stats[0:r, :, :].rearrange("p c n -> p (c n)")))
                v.tensor_scalar(nrm[0:r, 0:1], mv[0:r, 1:2], LN_EPS, None, ALU.add).then_inc(var_ready, 1)
                for c in range(2):
                    step(v.scalar_tensor_tensor(dst[:, c * 512:(c + 1) * 512], halves[c], mv[0:r, 0:1],
                                                ln_g[0:r, c * 512:(c + 1) * 512], ALU.subtract, ALU.mult))

            def norm_end(dst, r):
                count[1] += 1
                v.wait_ge(std_ready, count[1])
                link(v.reciprocal(nrm[0:r, 2:3], nrm[0:r, 1:2]))
                link(v.tensor_scalar(nrm[0:r, 3:4], nrm[0:r, 2:3], nrm[0:r, 2:3], nrm[0:r, 0:1], ALU.mult, ALU.mult))
                link(v.tensor_scalar(nrm[0:r, 4:5], nrm[0:r, 3:4], -0.5, 1.5, ALU.mult, ALU.add))
                link(v.tensor_scalar(nrm[0:r, 5:6], nrm[0:r, 4:5], nrm[0:r, 2:3], None, ALU.mult))
                v.scalar_tensor_tensor(dst[:, :], dst[:, :], nrm[0:r, 5:6], ln_b[0:r, :], ALU.mult,
                                       ALU.add).then_inc(ln_done, 1)
                v.wait_ge(ln_done, count[1])

            def layer_norm(dst, halves, r):
                norm_begin(dst, halves, r)
                norm_end(dst, r)

            link(v.memset(nrm[:, :], 1.0))
            v.wait_ge(ln_in[0], 32)
            for t in "MAB":
                n, r = rows[t]
                v.wait_ge(x_in[n], 16)
                src = h_meta if t == "M" else h[:, n, :]
                layer_norm(src, [src[:, 0:512], src[:, 512:1024]], r)

            def rope(src, dst, tab, r, hh, half):
                w = 2 * half
                t2 = tmp[0:r, 0:hh * w].rearrange("p (h d) -> p h d", h=hh)
                cos = tab[:, 0, :].unsqueeze(1).broadcast_to([r, hh, w])
                sin = tab[:, 1, :].unsqueeze(1).broadcast_to([r, hh, w])
                step(v.tensor_tensor(dst[:, :, 0:w], src[:, :, 0:w], cos, ALU.mult))
                step(v.tensor_tensor(t2[:, :, 0:half], src[:, :, half:w], sin[:, :, 0:half], ALU.mult))
                link(v.tensor_tensor(t2[:, :, half:w], src[:, :, 0:half], sin[:, :, half:w], ALU.mult))
                link(v.tensor_tensor(dst[:, :, 0:w], dst[:, :, 0:w], t2, ALU.add))

            v.wait_ge(const_in, 16 * N_CONST)

            def rope_index(n, r, src):
                hh = src.shape[1]
                dst = r_i[0:r, n, 5 - hh:5, :]
                step(v.tensor_copy(dst[:, :, 32:64], src[:, :, 32:64]))
                rope(src, dst, tabs_i[0:r, n, :, :], r, hh, 16)
                return v.tensor_copy(r_i[0:r, n, 5, :], r_i[0:r, n, 4, :])

            def rope_tile_index(t, nth):
                n, r = rows[t]
                wait_taken(v, "zs", t)
                rope_index(n, r, z[:, n, OFF_QI:OFF_QI + 320].rearrange("p (h d) -> p h d", d=DH)).then_inc(rotated, 1)
                v.wait_ge(rotated, nth)

            def rope_tile(t, nth):
                n, r = rows[t]
                wait_taken(v, "zq", t)
                rope(z[:, n, 0:640].rearrange("p (h d) -> p h d", d=DH), r_qk[:, n, :, :], tabs_q[:, n, :, :], r, 10, 32)
                v.tensor_copy(r_k[:, n, :, :, :], r_qk[:, n, 8:10, :].unsqueeze(2).broadcast_to([P, KV, 2, DH])).then_inc(rotated, 1)
                v.wait_ge(rotated, nth)

            rope_tile_index("A", 1)
            wait_taken(v, "zs", "M")
            M = N_META
            link(rope_index(2, M, z_m[0:M, 256:320].rearrange("p (h d) -> p h d", d=DH)))
            rope(z_m[0:M, 0:128].rearrange("p (h d) -> p h d", d=DH), r_mk[0:M, :, :], tabs_q[0:M, 2, :, :], M, KV, 32)
            v.tensor_copy(r_k[0:M, 2, :, :, :], r_mk[0:M, :, :].unsqueeze(2).broadcast_to([M, KV, 2, DH])).then_inc(rotated, 1)
            v.wait_ge(rotated, 2)
            rope_tile("A", 3)
            rope_tile_index("B", 4)
            rope_tile("B", 5)

            def select_keys(t):
                n = NK_OF[t]
                acc, left = isum[:, 0, 0:n], isum[:, 1, 0:n]
                mask = causal[:, t, 0:n]
                for hd in range(IH):
                    wait_full(v, "is", t, hd)
                    dst = rel[:, 0:n] if hd else acc
                    v.tensor_scalar(dst, bank("is", t, hd)[:, 0:n], 0.0, wi[:, t, hd:hd + 1], ALU.max,
                                    ALU.mult).then_inc(bank_taken["dve"], 1)
                    wait_taken(v, "is", t, hd)
                    if hd:
                        link(v.tensor_tensor(acc, acc, rel[:, 0:n], ALU.add))
                link(v.tensor_tensor(acc, acc, mask, ALU.add))
                cur, other = acc, left
                for _ in range(TOPK // 8):
                    link(v.max(m8[:, :], cur))
                    link(v.match_replace(other, m8[:, :], cur, NEG_TAKEN))
                    cur, other = other, cur
                link(v.tensor_scalar(cur, cur, -3.2e38, MASK, ALU.is_le, ALU.mult))
                link(v.tensor_scalar(mask, mask, -MASK / NEG_CAUSAL, -MASK, ALU.mult, ALU.add))
                link(v.tensor_tensor(mask, mask, cur, ALU.add))

            def softmax_input(t, hd):
                n = NK_OF[t]
                if hd == 0:
                    wait_full(v, *(("oT", 0) if t else ("qT", 1)))
                wait_full(v, "sc", t, hd)
                v.tensor_tensor_reduce(probs[:, hd, 0:n], bank("sc", t, hd)[:, 0:n], causal[:, t, 0:n], -SCALE, 3.0e38,
                                       ALU.add, ALU.min, neg_max[:, hd:hd + 1]).then_inc(bank_taken["dve"], 1)
                wait_taken(v, "sc", t, hd)
                v.sem_inc(scored, 1)

            def normalise(t):
                v.wait_ge(probs_ready, (t + 1) * HEADS)
                link(v.reciprocal(row_inv[:, :], row_sum[:, :]))
                wait_full(v, "pv", t)
                v.tensor_tensor(o_sb[:, :, :], bank("pv", t)[:, :].rearrange("p (h d) -> p h d", h=HEADS),
                                row_inv[:, :].unsqueeze(2).broadcast_to([P, HEADS, DH]), ALU.mult).then_inc(bank_taken["dve"], 1)
                wait_taken(v, "pv", t)
                v.sem_inc(o_ready, 1)

            def gate_pool(t, c):
                wait_full(v, "po", t, c)
                g = gT[:, t, 4 * c:4 * c + 4, :].rearrange("p c n -> p (c n)")
                v.tensor_tensor(g, g, bank("po", t, c)[:, :], ALU.mult).then_inc(bank_taken["dve"], 1)

            def gate_attention(t, c):
                wait_full(v, "ao", t, c)
                g = gT[:, t, KD + 4 * c:KD + 4 * c + 4, :].rearrange("p c n -> p (c n)")
                v.tensor_tensor(g, g, bank("ao", t, c)[:, :], ALU.mult).then_inc(bank_taken["dve"], 1)
                wait_taken(v, "ao", t, c)
                m = gT[:, t, 4 * c:4 * c + 4, :].rearrange("p c n -> p (c n)")
                v.tensor_tensor(m, m, g, ALU.add).then_inc(merged, 1)

            def residual(t, c):
                wait_full(v, "mx", t, c)
                hh = h[:, t, c * 512:(c + 1) * 512]
                v.scalar_tensor_tensor(hh, hh, ALPHA, bank("mx", t, c)[:, :], ALU.mult, ALU.add).then_inc(bank_taken["dve"], 1)
                wait_taken(v, "mx", t, c)

            def halves_of(t):
                return [h[:, t, c * 512:(c + 1) * 512] for c in range(2)]

            select_keys(0)
            for hd in range(HEADS):
                softmax_input(0, hd)
            select_keys(1)
            wait_taken(v, "gate", 3)
            for c in range(2):
                gate_pool(0, c)
            normalise(0)
            wait_taken(v, "gate", 7)
            for c in range(2):
                gate_attention(0, c)
            v.wait_ge(ln_in[1], 32)
            for c in range(2):
                residual(0, c)
            layer_norm(h[:, 0, :], halves_of(0), P)

            def topk(u, b):
                n = [0]

                def sig(i):
                    n[0] += 1
                    i.then_inc(topk_step, 1)

                def need(k):
                    v.wait_ge(topk_step, u * TOPK_STEPS + k)
                    if not isinstance(u, int):
                        v.sem_inc(topk_go, 1)

                v.wait_ge(s_loaded, u + 1)
                if not isinstance(u, int):
                    v.sem_inc(topk_go, 1)
                S = [s_cur[:, b, c, :] for c in range(2)]
                for c in range(2):
                    sig(v.max(top_v[:, c, 0:8], S[c]))
                for c in range(2):
                    need(1 + c)
                    sig(v.max_index(top_i[:, c, 0:8], top_v[:, c, 0:8], S[c]))
                for c in range(2):
                    sig(v.match_replace(s_left[:, c, :], top_v[:, c, 0:8], S[c], NEG_TAKEN))
                yield
                for c in range(2):
                    need(5 + c)
                    sig(v.max(top_v[:, c, 8:16], s_left[:, c, :]))
                for c in range(2):
                    need(7 + c)
                    sig(v.max_index(top_i[:, c, 8:16], top_v[:, c, 8:16], s_left[:, c, :]))
                sig(v.tensor_tensor(cand[:, :, :], top_v[:, 0, :].unsqueeze(2).broadcast_to([P, EK, EK]),
                                    top_v[:, 1, :].unsqueeze(1).broadcast_to([P, EK, EK]), ALU.add))
                flat = cand[:, :, :].rearrange("p a b -> p (a b)")
                need(11)
                sig(v.tensor_copy(top_if[:, :, :], top_i[:, :, :]))
                yield
                sig(v.max(best[:, b, 0:8], flat))
                need(13)
                sig(v.max_index(sel[:, 0:8], best[:, b, 0:8], flat))
                sig(v.match_replace(cand2[:, :], best[:, b, 0:8], flat, NEG_TAKEN))
                need(15)
                sig(v.max(best[:, b, 8:16], cand2[:, :]))
                need(16)
                sig(v.max_index(sel[:, 8:16], best[:, b, 8:16], cand2[:, :]))
                v.tensor_scalar(neg_top[:, b:b + 1], best[:, b, 0:1], -1.0, None, ALU.mult).then_inc(top_ready, 1)
                yield
                v.wait_ge(topk_step, u * TOPK_STEPS + 17)
                sig(v.tensor_scalar(ab[:, 0, :], sel[:, :], 4, None, ALU.logical_shift_right))
                sig(v.tensor_scalar(ab[:, 1, :], sel[:, :], 15, None, ALU.bitwise_and))
                v.wait_ge(topk_step, u * TOPK_STEPS + 19)
                sig(v.tensor_copy(abf[:, :, :], ab[:, :, :]))
                v.wait_ge(topk_step, u * TOPK_STEPS + 20)
                for c in range(2):
                    sig(v.tensor_tensor(hot[:, c, :, :], abf[:, c, :].unsqueeze(2).broadcast_to([P, EK, EK]),
                                        iota16[:, :].unsqueeze(1).broadcast_to([P, EK, EK]), ALU.is_equal))
                for c in range(2):
                    v.wait_ge(topk_step, u * TOPK_STEPS + 21 + c)
                    sig(v.tensor_tensor(hot[:, c, :, :], hot[:, c, :, :],
                                        top_if[:, c, :].unsqueeze(1).broadcast_to([P, EK, EK]), ALU.mult))
                yield
                v.wait_ge(topk_step, u * TOPK_STEPS + 24)
                v.tensor_reduce(pick[:, :, :], hot[:, :, :, :], AX_X, ALU.add).then_inc(ginv_ready, 1)
                v.wait_ge(ginv_ready, u + 1)
                v.scalar_tensor_tensor(expert[:, b, :], pick[:, 0, :], float(NK), pick[:, 1, :], ALU.mult,
                                       ALU.add).then_inc(idx_ready, 1)
                assert n[0] == TOPK_STEPS

            def weights_of(u, b, g):
                v.wait_ge(gelu_ready, u * GPU + g + 1)
                e = slice(g * GRP, (g + 1) * GRP)
                v.tensor_tensor(w_e[:, b, e], act_e[:, b, e], gate[:, b, e], ALU.mult).then_inc(w_ready, 1)

            def unit(u, t, b, nxt):
                v.wait_ge(gexp_ready, u + 1)
                v.reciprocal(ginv[:, b:b + 1], gsum[:, b:b + 1]).then_inc(gate_ready, 1)
                v.wait_ge(gate_ready, 2 * u + 1)
                v.tensor_scalar(gate[:, b, :], gexp[:, b, :], ginv[:, b:b + 1], None, ALU.mult).then_inc(gate_ready, 1)
                v.wait_ge(gate_ready, 2 * u + 2)
                best_of = topk(u + 2, b) if nxt else iter(())
                for g in range(GPU):
                    for i in range(GRP):
                        e = g * GRP + i
                        v.wait_ge(landed[e % RING], 16 * (u * (EK // RING) + e // RING + 1))
                        u_row = ring[:, e % RING, 0:D]
                        d = v.tensor_tensor_reduce(u_row, u_row, h[:, t, :], 1.0, 0.0, ALU.mult, ALU.add, dot[:, b, e:e + 1])
                    d.then_inc(dots_ready, 1)
                    if g:
                        weights_of(u, b, g - 1)
                    if g > LOAD_AT:
                        next(best_of, None)
                    if g < GPU - 1 and isinstance(u, int) and u < PH:
                        beside(u * GPU + g)
                weights_of(u, b, GPU - 1)
                if isinstance(u, int) and u < PH:
                    beside(u * GPU + GPU - 1)

            def beside(n):
                if 2 <= n < 6:
                    softmax_input(1, 2 * (n - 2))
                    softmax_input(1, 2 * (n - 2) + 1)
                if n == 17:
                    normalise(1)
                if n in (18, 20):
                    gate_pool(1, (n - 18) // 2)
                if n in (25, 27):
                    gate_attention(1, (n - 25) // 2)
                if n == 32:
                    residual(1, 0)
                if n == 35:
                    residual(1, 1)
                    norm_begin(h[:, 1, :], halves_of(1), P)
                if n == 37:
                    norm_end(h[:, 1, :], P)

            for b in range(2):
                for _ in topk(b, b):
                    pass

            def last_norm(t):
                v.wait_ge(ln_in[2], 32)
                v.wait_ge(group_free, AHEAD + (t + 1) * PH * GPU)
                layer_norm(h[:, t, :], [Y[t][0][:, :], Y[t][1][:, :]], P)

            for u in range(PH):
                unit(u, 0, u % 2, True)
            last_norm(0)
            with v.Fori(4, 7) as j:
                for b in range(2):
                    unit(2 * j + b, 1, b, True)
            for b in range(2):
                unit(UNITS - 2 + b, 1, b, False)
            last_norm(1)


def kernel(**inputs):
    import concourse.bacc as bacc
    from concourse.bass_utils import run_bass_kernel_spmd as run

    a = {k: np.asarray(v) for k, v in inputs.items()}
    nc = bacc.Bacc("TRN2", target_bir_lowering=False, num_devices=1)
    arrays, aps = {}, {}

    def give(name, value):
        value = np.ascontiguousarray(value)
        arrays[name] = value
        aps[name] = nc.dram_tensor(name, value.shape, mybir.dt.from_np(value.dtype), kind="ExternalInput").ap()

    def tables(rot):
        half = rot // 2
        inv = np.float32(10000.0) ** (-np.arange(half, dtype=np.float32) / np.float32(half))
        ang = np.arange(NPOS, dtype=np.float32)[:, None] * inv[None, :].astype(np.float32)
        cos, sin = np.cos(ang), np.sin(ang)
        return np.stack([np.concatenate([cos, cos], 1), np.concatenate([-sin, sin], 1)], 1).astype(np.float32)

    give("x", a["x"][0])
    give("meta", a["meta_tokens"])
    give("ln", np.stack([a["ln0_g"], a["ln0_b"], a["ln1_g"][0], a["ln1_b"][0], a["ln2_g"][0], a["ln2_b"][0]]))
    give("w_in", a["w_in"][0])
    give("b_gate_t", a["b_gate"][0].reshape(2 * KD, P).T)
    give("pool_w", a["pool_w"][0])
    give("pool_scale_t", a["pool_scale"][0].reshape(PG, P).T)
    give("w_pool_up", a["w_pool_up"][0])
    give("w_attn_o", a["w_attn_o"][0])
    give("w_out", a["w_out"][0])
    give("wq", a["peer_wq"][0])
    give("keys_t", a["peer_sub_keys"][0].reshape(2 * PH, NK, P).transpose(2, 0, 1))
    give("uv", np.concatenate([a["peer_u"][0], a["peer_v"][0]], axis=1))
    give("rope_q", tables(DH))
    give("rope_i", tables(32))
    give("ident_in", np.eye(P, dtype=np.float32))
    give("alpha_in", (np.eye(P) * ALPHA).astype(np.float32))
    give("iota_in", np.tile(np.arange(EK, dtype=np.float32), (P, 1)))
    q_pos = N_META + np.arange(SEQ)
    give("causal_in", np.where(np.arange(NPOS)[None, :] <= q_pos[:, None], 0.0, NEG_CAUSAL).astype(np.float32))
    out = nc.dram_tensor("out", (1, SEQ, D), F32, kind="ExternalOutput").ap()
    layer_kernel(nc, *aps.values(), out)
    r = run(nc, [arrays], core_ids=[0])
    return r.results[0]["out"]
```

```python
from contextlib import ExitStack

import concourse.bass as bass
import numpy as np
from concourse import mybir

ALU = mybir.AluOpType
ACT = mybir.ActivationFunctionType
AX_X = mybir.AxisListType.X
F32 = mybir.dt.float32
U32 = mybir.dt.uint32

P = 128
D = 1024
KD = D // P
N_META = 16
SEQ = 256
NPOS = N_META + SEQ
TILES = 2
PW = 512
PG = 4
WINDOWS = (2, 4, 8, 16)
HEADS, DH, KV = 8, 64, 2
IH = 4
QKVI = HEADS * DH + 2 * KV * DH + IH * DH + DH + IH
OFF_K, OFF_V, OFF_QI, OFF_KI, OFF_WI = 512, 640, 768, 1024, 1088
TOPK = 64
SCALE = DH ** -0.5
PH = 8
EK = 16
NK = 128
LN_EPS = 1e-5
ALPHA = 2.0 ** 0.25
NEG_CAUSAL = -3.0e38
NEG_TAKEN = -3.4e38
MASK = 1.0e30
RING = 8
GRP = 2
GPU = EK // GRP
AHEAD = RING // GRP
UNITS = TILES * PH
WARM_UP = 5
GROUPS = [(g, range(g * GRP, (g + 1) * GRP)) for g in range(GPU)]
LAST_GROUPS = GROUPS[:-1] + [(GPU - 1 + i, [EK - GRP + i]) for i in range(GRP)]
LOAD_AT = 2
TOPK_STEPS = 24
SLOT = 4096
NK_OF = (N_META + P, NPOS)
POS = (N_META, N_META + P)


QUERY_BLOCKS = ([(0, 2), (2, 2), (4, 4), (8, 4), (12, 4)], [(0, 4), (4, 4), (8, 4), (12, 4)])


def block_of(u):
    return u // PH, max(n for n, _ in QUERY_BLOCKS[u // PH] if n <= 2 * (u % PH))


def bank_jobs():
    first = [("hT", "A", c) for c in range(2)] + [("zk", "A"), ("hT", "M", 0), ("zs", "A")]
    first += [("zk", "M"), ("zs", "M")]
    first += [("hT", "B", c) for c in range(2)] + [("zq", "A")] + [(z, "B") for z in ("zk", "zs", "zq")]
    first += [("iT", "A"), ("mT",)] + [("xp", g) for g in range(PG)]
    first += [("is", 0, h) for h in range(IH)]
    first += [("qT", 0), ("iT", "B"), ("kT",), ("qT", 1)]
    first += [("gate", c) for c in range(3)]
    first += [("sc", 0, h) for h in range(HEADS)]
    first += [("gate", 3)] + [("yT", c) for c in range(2)]
    first += [("is", 1, h) for h in range(IH)]
    first += [("po", 0, c) for c in range(2)]
    first += [("pm", 0, c) for c in range(2)] + [("pk", 0, c) for c in range(2)]
    first += [("ga", 0, 0), ("pv", 0), ("ga", 0, 1), ("oT", 0)] + [("ao", 0, c) for c in range(2)]
    first += [("mx", 0, c) for c in range(2)] + [("po", 1, c) for c in range(2)]
    first += [("h1T", 0, c) for c in range(2)]
    first += [("q2", 0, 0), ("ss", 0, 0), ("q2", 0, 2), ("q2", 0, 4), ("ss", 0, 2), ("q2", 0, 8), ("ss", 0, 4)]
    first += [("q2", 0, 12)]
    beside = [("ss", 0, 8), ("ss", 0, 12)] + [("sc", 1, h) for h in range(HEADS)] + [("ga", 1, 0)]
    beside += [("pm", 1, c) for c in range(2)] + [("pk", 1, c) for c in range(4)]
    beside += [("pv", 1), ("ga", 1, 1), ("oT", 1)] + [("ao", 1, c) for c in range(2)]
    beside += [("mx", 1, c) for c in range(2)] + [("h1T", 1, c) for c in range(2)]
    beside += [("ln2", c) for c in range(4)]
    for n, _ in QUERY_BLOCKS[1]:
        beside += [("q2", 1, n), ("ss", 1, n)]
    dve = ("is", "sc", "po", "pv", "ao", "mx")
    jobs = [(j, "dve" if j[0] in dve else "act") for j in first + beside]
    at = [n % 8 for n in range(len(first))] + [n % 4 for n in range(len(beside))]
    return jobs, at


JOBS, BANK_AT = bank_jobs()
JOB_AT = {j: n for n, (j, _) in enumerate(JOBS)}


def taken_before(n, who):
    return sum(w == who for _, w in JOBS[:n])


CHUNKS = [("kvqi", 2, ("zk", "B")), ("q", 3, ("zq", "B")), ("xp", 0, ("xp", 3)),
          ("g0", 1, ("gate", 1)), ("g2", 4, ("ga", 1, 0)), ("g3", 5, ("ga", 1, 1)), ("g1", 2, ("gate", 3)),
          ("pool_up", 3, ("po", 1, 1)), ("attn_o", 0, ("ao", 0, 1)),
          ("out0", 1, ("mx", 0, 0)), ("out1", 2, ("mx", 0, 1)), ("wq0", 0, ("q2", 0, 2)),
          ("wq1", 1, ("q2", 0, 4)), ("wq2", 2, ("q2", 0, 8)), ("wq3", 3, ("q2", 0, 12)),
          ("attn_o again", 4, ("ao", 1, 1)), ("out0 again", 5, ("mx", 1, 0)), ("out1 again", 4, ("mx", 1, 1)),
          *((f"wq{c} again", 5 - c % 2, ("q2", 1, 4 * c)) for c in range(4))]
SLOT_OF = {c: s for c, s, _ in CHUNKS}


def slot_uses(name):
    n = [c for c, *_ in CHUNKS].index(name)
    return sum(s == SLOT_OF[name] for _, s, _ in CHUNKS[:n + 1])


def layer_kernel(nc, x, meta, ln, w_in, b_gate_t, pool_w, pool_scale_t, w_pool_up, w_attn_o, w_out,
                 wq, keys_t, uv, rope_q, rope_i, ident_in, alpha_in, iota_in, causal_in, out):
    with ExitStack() as ctx:
        def sb(name, shape, dt=F32):
            return ctx.enter_context(nc.sbuf_tensor(name, shape, dt))

        def sem(name):
            return ctx.enter_context(nc.semaphore(name))

        weights = sb("weights", [P, 6 * SLOT])
        ring = weights[:, 0:4 * SLOT].rearrange("p (s n) -> p s n", s=RING)
        h = sb("h", [P, TILES, D])
        h_meta = weights[0:N_META, 5 * SLOT:5 * SLOT + D]
        hT = sb("hT", [P, TILES, KD, N_META + P])
        h1T = hT[:, :, :, :].rearrange("p t k n -> p t (k n)")[:, :, 0:D].rearrange("p t (k n) -> p t k n", k=KD)
        ln_g = sb("ln_g", [P, D])
        ln_b = sb("ln_b", [P, D])
        gT = sb("gT", [P, TILES, 2 * KD, P])
        q2T = gT
        arena = sb("arena", [P, 10368])
        z = arena[:, 0:2184].rearrange("p (t n) -> p t n", t=TILES)
        z_m = arena[:, 2184:2508]
        r_qk = arena[:, 2508:3788].rearrange("p (t h d) -> p t h d", t=TILES, d=DH)
        r_k = arena[:, 3788:4556].rearrange("p (t g c d) -> p t g c d", t=3, g=KV, c=2)
        r_i = arena[:, 4556:5708].rearrange("p (t h d) -> p t h d", t=3, d=DH)
        r_mk = arena[:, 5708:5836].rearrange("p (h d) -> p h d", d=DH)
        tmp = arena[:, 5836:6476]
        tabs_q = arena[:, 6476:6860].rearrange("p (t c d) -> p t c d", t=3, c=2)
        tabs_i = arena[:, 6860:7052].rearrange("p (t c d) -> p t c d", t=3, c=2)
        xpT = arena[:, 7052:8140].rearrange("p (g n) -> p g n", g=PG)
        wsum = arena[:, 8140:8684].rearrange("p (c n) -> p c n", c=2)
        pw = arena[:, 8684:9196].rearrange("p (g n) -> p g n", g=PG)
        w_small = arena[:, 9196:9740].rearrange("p (k n) -> p k n", k=KD)
        probs = arena[:, 0:2176].rearrange("p (h n) -> p h n", h=HEADS)
        o_sb = arena[:, 0:HEADS * DH].rearrange("p (h d) -> p h d", h=HEADS)
        pT_meta = arena[:, 2176:3200].rearrange("p (h n) -> p h n", h=HEADS)
        pT = arena[:, 3200:5248].rearrange("p (h c n) -> p h c n", h=HEADS, c=2)
        s_all = arena[:, 5248:7296].rearrange("p (u n) -> p u n", u=PH)
        diag = arena[:, 7296:8320].rearrange("p (s n) -> p s n", s=RING)
        keysT = arena[:, 8320:10368].rearrange("p (c n) -> p c n", c=2 * PH)
        ln2_row = arena[0:1, 0:2 * D]
        ones = arena[0:1, 2 * D:2 * D + P]
        wi = sb("wi", [P, TILES, IH])
        v_sb = sb("v_sb", [P, 3, KV * DH])
        iT = sb("iT", [P, TILES, 2, P])
        kiT = sb("kiT", [P, NPOS])
        qT = sb("qT", [P, TILES, 4, P])
        kT = sb("kT", [P, KV, NPOS])
        rel = sb("rel", [P, NPOS])
        isum = sb("isum", [P, 2, NPOS])
        causal = sb("causal", [P, TILES, NPOS])
        m8 = sb("m8", [P, 8])
        neg_max = sb("neg_max", [P, HEADS])
        row_sum = sb("row_sum", [P, HEADS])
        row_inv = sb("row_inv", [P, HEADS])
        oT = sb("oT", [P, TILES, 4, P])
        yT = oT
        ident = sb("ident", [P, P])
        alpha_i = sb("alpha_i", [P, P])
        iota16 = sb("iota16", [P, EK])
        bg = sb("bg", [P, 2 * KD])
        ps = sb("ps", [P, PG])
        stats = sb("stats", [P, 2, 6])
        mv = sb("mv", [P, 2])
        nrm = sb("nrm", [P, 8])
        s_cur = sb("s_cur", [P, 2, 2, NK])
        s_left = sb("s_left", [P, 2, NK])
        top_v = sb("top_v", [P, 2, EK])
        top_i = sb("top_i", [P, 2, EK], U32)
        top_if = sb("top_if", [P, 2, EK])
        cand = sb("cand", [P, EK, EK])
        cand2 = sb("cand2", [P, EK * EK])
        best = sb("best", [P, 2, EK])
        sel = sb("sel", [P, EK], U32)
        ab = sb("ab", [P, 2, EK], U32)
        abf = sb("abf", [P, 2, EK])
        hot = sb("hot", [P, 2, EK, EK])
        pick = sb("pick", [P, 2, EK])
        expert = sb("expert", [P, 2, EK], U32)
        neg_top = sb("neg_top", [P, 2])
        gexp = sb("gexp", [P, 2, EK])
        gsum = sb("gsum", [P, 2])
        ginv = sb("ginv", [P, 2])
        gate = sb("gate", [P, 2, EK])
        dot = sb("dot", [P, 2, EK])
        act_e = sb("act_e", [P, 2, EK])
        w_e = sb("w_e", [P, 2, EK])

        banks = [ctx.enter_context(nc.psum_tensor(f"bank{n}", [P, 512], F32)) for n in range(8)]
        Y = [(banks[4], banks[5]), (banks[6], banks[7])]

        x_in = [sem(f"x_in_{t}") for t in "ABM"]
        ln_g_in = [sem(f"ln{n}_g_in") for n in range(2)]
        ln_b_in = [sem(f"ln{n}_b_in") for n in range(2)]
        ln2_spread = sem("ln2_spread")
        pad_ready = sem("pad_ready")
        zeros_ready = sem("zeros_ready")
        const_in = sem("const_in")
        ident_sem = sem("ident_in")
        small_in = sem("small_in")
        keys_in = sem("keys_in")
        slot_in = [sem(f"slot_in{s}") for s in range(6)]
        first_half_in = sem("first_half_in")
        ln2_in = sem("ln2_in")
        ones_ready = sem("ones_ready")
        bank_full = sem("bank_full")
        bank_taken = {"act": sem("bank_taken_act"), "dve": sem("bank_taken_dve")}
        dve_step = sem("dve_step")
        pool_step = sem("pool_step")
        var_ready = sem("var_ready")
        std_ready = sem("std_ready")
        ln_half = sem("ln_half")
        ln_done = sem("ln_done")
        rotated = sem("rotated")
        scored = sem("scored")
        probs_ready = sem("probs_ready")
        o_ready = sem("o_ready")
        merged = sem("merged")
        windows_done = sem("windows_done")
        s_loaded = sem("s_loaded")
        topk_step = sem("topk_step")
        idx_ready = sem("idx_ready")
        top_ready = sem("top_ready")
        gexp_ready = sem("gexp_ready")
        pick_ready = sem("pick_ready")
        gate_ready = sem("gate_ready")
        landed = [sem(f"landed{s}") for s in range(RING)]
        dots_ready = sem("dots_ready")
        gelu_ready = sem("gelu_ready")
        w_ready = sem("w_ready")
        diag_ready = sem("diag_ready")
        group_free = sem("group_free")
        y_ready = sem("y_ready")
        out_done = sem("out_done")
        dve_passed, act_passed, pool_passed = (sem(f"{e}_passed") for e in ("dve", "act", "pool"))

        def bank(*job):
            return banks[BANK_AT[JOB_AT[job]]]

        def wait_free(pe, *job):
            n = JOB_AT[job]
            older = [m for m in range(n) if BANK_AT[m] == BANK_AT[n]]
            if older:
                wait_taken(pe, *JOBS[older[-1]][0])

        def wait_full(eng, *job):
            eng.wait_ge(bank_full, JOB_AT[job] + 1)

        def wait_taken(eng, *job):
            n = JOB_AT[job]
            who = JOBS[n][1]
            eng.wait_ge(bank_taken[who], taken_before(n, who) + 1)

        def chunk(name, k):
            s = SLOT_OF[name]
            return weights[:, s * SLOT:(s + 1) * SLOT].rearrange("p (k n) -> p k n", k=k)

        def wait_chunk(pe, name):
            pe.wait_ge(slot_in[SLOT_OF[name]], 16 * slot_uses(name))

        def stream(t):
            return hT[:, 0, :, 0:N_META] if t == "M" else hT[:, "AB".index(t), :, N_META:N_META + P]

        rows = {"A": (0, P), "B": (1, P), "M": (2, N_META)}
        where = {"M": 0, "A": POS[0], "B": POS[1]}
        w_in_k = w_in.rearrange("(k p) n -> p k n", p=P)
        SRC = {
            "kvqi": w_in_k[:, :, PW + OFF_K:PW + OFF_K + 512], "q": w_in_k[:, :, PW:PW + 512],
            "xp": w_in_k[:, :, 0:PW],
            **{f"g{c}": w_in_k[:, :, PW + QKVI + 512 * c:PW + QKVI + 512 * c + 512] for c in range(4)},
            "pool_up": w_pool_up.rearrange("(k p) n -> p k n", p=P),
            "attn_o": w_attn_o.rearrange("(k p) n -> p k n", p=P),
            **{f"out{c}": w_out.rearrange("(k p) n -> p k n", p=P)[:, :, 512 * c:512 * c + 512] for c in range(2)},
            **{f"wq{c}": wq.rearrange("(k p) n -> p k n", p=P)[:, :, 512 * c:512 * c + 512] for c in range(4)},
        }
        SRC.update({f"{name} again": src for name, src in SRC.items()})

        N_CONST = 12

        block = ctx.enter_context(nc.Block())

        @block.sync
        def _(sp):
            def load_ln(n):
                sp.dma_start(ln_g[:, :], ln[2 * n:2 * n + 1, :].partition_broadcast(P)).then_inc(ln_g_in[n], 16)
                sp.dma_start(ln_b[:, :], ln[2 * n + 1:2 * n + 2, :].partition_broadcast(P)).then_inc(ln_b_in[n], 16)

            def load_chunk(n):
                name, s, _ = CHUNKS[n]
                if name == "g3":
                    wait_full(sp, "hT", "M", 0)
                older = [last for _, t, last in CHUNKS[:n] if t == s]
                if older:
                    wait_full(sp, *older[-1])
                k = SRC[name].shape[1]
                if n == 0:
                    sp.dma_start(chunk(name, k)[:, 0:k // 2, :], SRC[name][:, 0:k // 2, :]).then_inc(first_half_in, 16)
                    sp.dma_start(chunk(name, k)[:, k // 2:k, :], SRC[name][:, k // 2:k, :]).then_inc(slot_in[s], 16)
                else:
                    sp.dma_start(chunk(name, k), SRC[name]).then_inc(slot_in[s], 16)

            sp.dma_start(h[:, 0, :], x[0:P, :]).then_inc(x_in[0], 16)
            load_ln(0)
            sp.dma_start(h_meta, meta).then_inc(x_in[2], 16)
            sp.dma_start(ident[:, :], ident_in).then_inc(ident_sem, 16)
            load_chunk(0)
            sp.dma_start(w_small, w_in_k[:, :, PW + OFF_KI:PW + QKVI]).then_inc(small_in, 16)
            sp.dma_start(h[:, 1, :], x[P:SEQ, :]).then_inc(x_in[1], 16)
            for t, (n, rows_) in rows.items():
                r = where[t]
                sp.dma_start(tabs_q[0:rows_, n, :, :], rope_q[r:r + rows_]).then_inc(const_in, 16)
                sp.dma_start(tabs_i[0:rows_, n, :, :], rope_i[r:r + rows_]).then_inc(const_in, 16)
            load_chunk(1)
            load_chunk(2)
            sp.dma_start(causal[:, :, :], causal_in.rearrange("(t p) n -> p t n", p=P)).then_inc(const_in, 16)
            sp.dma_start(bg[:, :], b_gate_t).then_inc(const_in, 16)
            sp.dma_start(ps[:, :], pool_scale_t).then_inc(const_in, 16)
            sp.dma_start(iota16[:, :], iota_in).then_inc(const_in, 16)
            sp.dma_start(alpha_i[:, :], alpha_in).then_inc(const_in, 16)
            sp.dma_start(pw[:, :, :], pool_w.rearrange("g c d -> c g d")).then_inc(const_in, 16)
            for n in range(3, 6):
                load_chunk(n)
            sp.wait_ge(ln_done, 3)
            load_ln(1)
            for n in range(6, len(CHUNKS)):
                if CHUNKS[n][0] == "wq0":
                    wait_full(sp, "yT", 1)
                    sp.dma_start(keysT[:, :, :], keys_t).then_inc(keys_in, 16)
                if CHUNKS[n][0] == "wq0 again":
                    wait_full(sp, "mx", 1, 1)
                    sp.dma_start(ln2_row, ln[4:6, :].rearrange("(o a) n -> o (a n)", o=1)).then_inc(ln2_in, 16)
                load_chunk(n)
            for t in range(TILES):
                for c, ready in enumerate((ln_half, ln_done)):
                    sp.wait_ge(ready, 6 + t)
                    cols = slice(c * 512, (c + 1) * 512)
                    sp.dma_start(out[0, t * P:(t + 1) * P, cols], h[:, t, cols]).then_inc(out_done, 16)
            sp.wait_ge(out_done, 16 * 2 * TILES)

        @block.gpsimd
        def _(pool):
            steps = 0
            for g, w in enumerate(WINDOWS):
                wait_taken(pool, "xp", g)
                src, width, first = xpT[:, g, :], 1, 0
                n = 0
                while width < w:
                    first += width
                    dst = wsum[:, n % 2, :]
                    pool.tensor_tensor(dst[:, first:NPOS], src[:, first:NPOS], src[:, first - width:NPOS - width],
                                       ALU.add).then_inc(pool_step, 1)
                    steps += 1
                    pool.wait_ge(pool_step, steps)
                    src, width, n = dst, 2 * width, n + 1
                pool.tensor_scalar(src[:, N_META:NPOS], src[:, N_META:NPOS], 1.0 / w, None, ALU.mult).then_inc(pool_step, 1)
                steps += 1
                pool.wait_ge(pool_step, steps)
                pool.tensor_tensor(xpT[:, g, N_META:NPOS], src[:, N_META:NPOS], xpT[:, g, N_META:NPOS],
                                   ALU.subtract).then_inc(windows_done, 1)
                pool.wait_ge(windows_done, g + 1)

            def gather_unit(u, b):
                pool.wait_ge(idx_ready, u + 1)
                for e in range(EK):
                    if e % GRP == 0:
                        pool.wait_ge(group_free, u * GPU + e // GRP + 1)
                        pool.sem_inc(pool_passed, 1)
                    pool.indirect_dma_start(ring[:, e % RING, :], None, uv,
                                            bass.IndirectOffsetOnAxis(ap=expert[:, b, e:e + 1], axis=0)
                                            ).then_inc(landed[e % RING], 16)

            with pool.Fori(0, UNITS // 2) as j:
                for b in range(2):
                    gather_unit(2 * j + b, b)

        @block.scalar
        def _(act):
            def take(dst, src, last=True, **kw):
                i = act.activation(dst, src, kw.pop("func", ACT.Copy), **kw)
                if last:
                    i.then_inc(bank_taken["act"], 1)
                return i

            def std(n):
                act.wait_ge(var_ready, n)
                act.activation(nrm[:, 1:2], nrm[:, 0:1], ACT.Sqrt).then_inc(std_ready, 1)

            def take_h(t):
                n, r = rows[t]
                for c in range(1 if t == "M" else 2):
                    wait_full(act, "hT", t, c)
                    kk = KD if t == "M" else 4
                    take(stream(t)[:, c * 4:c * 4 + kk, :],
                         bank("hT", t, c)[:, 0:kk * r].rearrange("p (k n) -> p k n", k=kk))

            def take_z(kind, t):
                n, r = rows[t]
                wait_full(act, kind, t)
                src = bank(kind, t)
                if kind == "zk":
                    take(v_sb[0:r, n, :], src[0:r, 128:256], last=False)
                    if t == "M":
                        take(z_m[0:r, 0:256], src[0:r, 0:256])
                    else:
                        take(z[:, n, OFF_K:OFF_K + 512], src[:, :])
                elif kind == "zq":
                    take(z[:, n, 0:512], src[:, :])
                elif t == "M":
                    take(z_m[0:r, 256:320], src[0:r, 0:64])
                else:
                    take(wi[:, n, :], src[:, 64:68], last=False, scale=IH ** -0.5 * DH ** -0.5)
                    take(z[:, n, OFF_KI:QKVI], src[:, 0:68])

            def take_index(t):
                n, _ = rows[t]
                wait_full(act, "iT", t)
                src = bank("iT", t)
                take(iT[:, n, :, :], src[:, 0:2 * P].rearrange("p (c n) -> p c n", c=2), last=False)
                take(kiT[:, where[t]:where[t] + P], src[:, 2 * P:3 * P])

            def take_queries(t):
                wait_full(act, "qT", t)
                take(qT[:, t, :, :], bank("qT", t)[:, :].rearrange("p (c n) -> p c n", c=4))

            def take_gates(c):
                wait_full(act, "gate", c)
                for i in range(2):
                    take(gT[:, :, 2 * c + i, :], bank("gate", c)[:, i * SEQ:(i + 1) * SEQ].rearrange("p (t n) -> p t n", t=TILES),
                         func=ACT.Sigmoid, bias=bg[:, 2 * c + i:2 * c + i + 1], last=(i == 1))

            def take_attention_gates(t, c):
                wait_full(act, "ga", t, c)
                for i in range(4):
                    n = KD + 4 * c + i
                    take(gT[:, t, n, :], bank("ga", t, c)[:, i * P:(i + 1) * P], func=ACT.Sigmoid,
                         bias=bg[:, n:n + 1], last=(i == 3))

            def exp_scores(t):
                for hd in range(HEADS):
                    act.wait_ge(scored, t * HEADS + hd + 1)
                    act.activation(probs[:, hd, 0:NK_OF[t]], probs[:, hd, 0:NK_OF[t]], ACT.Exp,
                                   bias=neg_max[:, hd:hd + 1], scale=-1.0,
                                   accum_out=row_sum[:, hd:hd + 1]).then_inc(probs_ready, 1)

            def take_meta_probs(t, c):
                wait_full(act, "pm", t, c)
                take(pT_meta[0:N_META, 4 * c:4 * c + 4, :],
                     bank("pm", t, c)[0:N_META, :].rearrange("p (h n) -> p h n", h=4))

            def take_probs(t, c):
                wait_full(act, "pk", t, c)
                if t == 0:
                    take(pT[:, 4 * c:4 * c + 4, 0, :], bank("pk", t, c)[:, :].rearrange("p (h n) -> p h n", h=4))
                else:
                    take(pT[:, 2 * c:2 * c + 2, :, :],
                         bank("pk", t, c)[:, :].rearrange("p (h c n) -> p h c n", h=2, c=2))

            def take_block(name, t, c, dst):
                wait_full(act, name, t, c)
                take(dst[:, t, 4 * c:4 * c + 4, :], bank(name, t, c)[:, :].rearrange("p (k n) -> p k n", k=4))

            def take_o(t):
                wait_full(act, "oT", t)
                take(oT[:, t, :, :], bank("oT", t)[:, :].rearrange("p (c n) -> p c n", c=4))

            def take_queries2(t, n):
                count = dict(QUERY_BLOCKS[t])[n]
                wait_full(act, "q2", t, n)
                take(q2T[:, t, n:n + count, :], bank("q2", t, n)[:, 0:count * P].rearrange("p (k n) -> p k n", k=count))

            def take_ss(t, n):
                heads = dict(QUERY_BLOCKS[t])[n] // 2
                wait_full(act, "ss", t, n)
                if t:
                    act.wait_ge(s_loaded, PH)
                take(s_all[:, n // 2:n // 2 + heads, :],
                     bank("ss", t, n)[:, 0:heads * 2 * NK].rearrange("p (u n) -> p u n", u=heads))

            def take_first_ss(u):
                wait_full(act, "ss", 0, 2 * u)
                take(s_cur[:, u, :, :].rearrange("p c n -> p (c n)"), bank("ss", 0, 2 * u)[:, 0:2 * NK])
                wait_taken(act, "ss", 0, 2 * u)
                act.sem_inc(s_loaded, 1)

            std(1)
            take_h("A")
            std(2)
            std(3)
            take_z("zk", "A")
            take_h("M")
            take_z("zs", "A")
            for kind in ("zk", "zs"):
                take_z(kind, "M")
            take_h("B")
            take_z("zq", "A")
            for kind in ("zk", "zs", "zq"):
                take_z(kind, "B")
            take_index("A")
            wait_full(act, "mT")
            src = bank("mT")
            take(kiT[:, 0:N_META], src[:, 0:N_META], last=False)
            take(kT[:, :, 0:N_META], src[:, N_META:3 * N_META].rearrange("p (g n) -> p g n", g=KV))
            for g in range(PG):
                wait_full(act, "xp", g)
                take(xpT[:, g, 0:POS[1]], bank("xp", g)[:, 0:POS[1]], last=False)
                take(xpT[:, g, POS[1]:NPOS], bank("xp", g)[:, N_META + POS[1]:N_META + NPOS])
            take_queries(0)
            take_index("B")
            wait_full(act, "kT")
            for t in range(TILES):
                take(kT[:, :, POS[t]:POS[t] + P],
                     bank("kT")[:, t * 256:t * 256 + 256].rearrange("p (g n) -> p g n", g=KV), last=(t == 1))
            take_queries(1)
            act.wait_ge(const_in, 16 * N_CONST)
            for c in range(3):
                take_gates(c)
            exp_scores(0)
            take_gates(3)
            for c in range(2):
                wait_full(act, "yT", c)
                for i in range(2):
                    g = 2 * c + i
                    take(yT[:, :, g, :], bank("yT", c)[:, i * SEQ:(i + 1) * SEQ].rearrange("p (t n) -> p t n", t=TILES),
                         scale=ps[:, g:g + 1], last=(i == 1))
            for c in range(2):
                take_meta_probs(0, c)
            for c in range(2):
                take_probs(0, c)
            for c in range(2):
                take_attention_gates(0, c)
            take_o(0)
            std(4)
            for c in range(2):
                take_block("h1T", 0, c, h1T)

            def exp_gates(u, b):
                act.wait_ge(top_ready, u + 1)
                act.activation(gexp[:, b, :], best[:, b, :], ACT.Exp, bias=neg_top[:, b:b + 1],
                               accum_out=gsum[:, b:b + 1]).then_inc(gexp_ready, 1)

            def load_scores(u, b):
                act.activation(s_cur[:, b, :, :].rearrange("p c n -> p (c n)"), s_all[:, u, :],
                               ACT.Copy).then_inc(s_loaded, 1)

            take_queries2(0, 0)
            take_first_ss(0)
            take_queries2(0, 2)
            take_queries2(0, 4)
            take_first_ss(1)
            exp_gates(0, 0)
            take_queries2(0, 8)
            take_ss(0, 4)
            exp_gates(1, 1)

            def beside(n):
                if n == 0:
                    take_queries2(0, 12)
                if n == 2:
                    take_ss(0, 8)
                    take_ss(0, 12)
                if n == 7:
                    exp_scores(1)
                if n == 10:
                    take_attention_gates(1, 0)
                if n == 11:
                    take_meta_probs(1, 0)
                    take_meta_probs(1, 1)
                if n == 13:
                    take_probs(1, 0)
                    take_probs(1, 1)
                if n == 14:
                    take_probs(1, 2)
                    take_probs(1, 3)
                if n == 20:
                    take_attention_gates(1, 1)
                if n == 22:
                    take_o(1)
                if n == 37:
                    std(5)
                if n == 42:
                    for c in range(2):
                        take_block("h1T", 1, c, h1T)
                if n == 44:
                    act.wait_ge(ln_done, 5)
                    for c in range(4):
                        wait_full(act, "ln2", c)
                        take((ln_g, ln_b)[c // 2][:, c % 2 * 512:c % 2 * 512 + 512], bank("ln2", c)[:, :])
                        wait_taken(act, "ln2", c)
                        act.sem_inc(ln2_spread, 1)
                if n in (47, 52, 57, 61):
                    take_queries2(1, 4 * (47, 52, 57, 61).index(n))
                if n in (50, 55, 60, 63):
                    take_ss(1, 4 * (50, 55, 60, 63).index(n))

            def unit(u, b, score_row, groups=GROUPS):
                for g, experts in groups:
                    act.wait_ge(dots_ready, u * GPU + g + 1)
                    e = slice(experts[0], experts[-1] + 1)
                    act.activation(act_e[:, b, e], dot[:, b, e], ACT.Gelu).then_inc(gelu_ready, 1)
                    act.wait_ge(group_free, u * GPU + min(g, GPU - 1) + 1)
                    act.wait_ge(w_ready, u * GPU + g + 1)
                    for e in experts:
                        d = act.activation(diag[:, e % RING, :], ident[:, :], ACT.Copy, scale=w_e[:, b, e:e + 1])
                    d.then_inc(diag_ready, 1)
                    if isinstance(u, int) and u < PH:
                        beside(u * GPU + g)
                    if isinstance(u, int) and u == UNITS - 2 and g == 1:
                        std(6)
                    if g == LOAD_AT and score_row is not None:
                        act.wait_ge(top_ready, u + 1)
                        if isinstance(u, int):
                            wait_taken(act, "ss", *block_of(u + 2))
                        else:
                            act.sem_inc(act_passed, 1)
                        load_scores(score_row, b)

            for u in range(PH):
                unit(u, u % 2, (u + 2) % PH)
                exp_gates(u + 2, u % 2)
            wait_taken(act, "ss", 1, 12)
            with act.Fori(4, 7) as j:
                for b in range(2):
                    u = 2 * j + b
                    unit(u, b, u + 2 - PH)
                    exp_gates(u + 2, b)
            unit(UNITS - 2, 0, None)
            unit(UNITS - 1, 1, None, LAST_GROUPS)
            std(7)

        @block.tensor
        def _(pe):
            def full(mm):
                mm.then_inc(bank_full, 1)

            def stream_t(t):
                n, r = rows[t]
                src = h_meta if t == "M" else h[:, n, :]
                pe.wait_ge(ln_half, "AMB".index(t) + 1)
                for c in range(1 if t == "M" else 2):
                    if c or t == "M":
                        pe.wait_ge(ln_done, "AMB".index(t) + 1)
                    wait_free(pe, "hT", t, c)
                    kk = KD if t == "M" else 4
                    for k in range(kk):
                        mm = pe.transpose(bank("hT", t, c)[:, k * r:(k + 1) * r],
                                          src[:, (4 * c + k) * P:(4 * c + k + 1) * P], ident[0:r, 0:r])
                    full(mm)

            def project(job, t, w, cols):
                n, r = rows[t]
                wait_free(pe, *job)
                for k in range(KD):
                    if job == ("zk", "A") and k == 0:
                        wait_taken(pe, "hT", "A", 0)
                        pe.wait_ge(first_half_in, 16)
                    if job == ("zk", "A") and k == KD // 2:
                        wait_taken(pe, "hT", "A", 1)
                        wait_chunk(pe, "kvqi")
                    mm = pe.matmul(bank(*job)[0:r, 0:cols], stream(t)[:, k, :], w[:, k, 0:cols],
                                   start=(k == 0), stop=(k == KD - 1))
                full(mm)

            def project_z(kind, t):
                cols = {"zk": 256 if t == "M" else 512, "zs": 64 if t == "M" else 68, "zq": 512}[kind]
                w = {"zk": chunk("kvqi", KD), "zs": w_small, "zq": chunk("q", KD)}[kind]
                project((kind, t), t, w, cols)

            pe.wait_ge(zeros_ready, 1)
            for _ in range(WARM_UP):
                pe.matmul(banks[7][:, :], arena[:, 0:P], arena[:, 0:512], start=True, stop=True)
            pe.wait_ge(ident_sem, 16)
            stream_t("A")
            project_z("zk", "A")
            stream_t("M")
            pe.wait_ge(small_in, 16)
            project_z("zs", "A")
            wait_taken(pe, "hT", "M", 0)
            project_z("zk", "M")
            project_z("zs", "M")
            stream_t("B")
            wait_chunk(pe, "q")
            project_z("zq", "A")
            wait_taken(pe, "hT", "B", 1)
            for kind in ("zk", "zs", "zq"):
                project_z(kind, "B")

            def pool_inputs():
                wait_chunk(pe, "xp")
                pe.wait_ge(pad_ready, 1)
                for g in range(PG):
                    wait_free(pe, "xp", g)
                    for k in range(KD):
                        mm = pe.matmul(bank("xp", g)[:, 0:N_META + NPOS].rearrange("p (t n) -> p t n", t=TILES),
                                       chunk("xp", KD)[:, k, g * P:(g + 1) * P], hT[:, :, k, :],
                                       start=(k == 0), stop=(k == KD - 1))
                    full(mm)

            def transposes(job, srcs, r=P):
                wait_free(pe, *job)
                for i, s in enumerate(srcs):
                    mm = pe.transpose(bank(*job)[:, i * r:(i + 1) * r], s, ident[0:r, 0:r])
                full(mm)

            def transpose_index(t):
                transposes(("iT", t), [r_i[:, rows[t][0], 2 * c:2 * c + 2, :].rearrange("p h d -> p (h d)") for c in range(3)])

            def transpose_queries(t):
                transposes(("qT", t), [r_qk[:, t, 2 * c:2 * c + 2, :].rearrange("p h d -> p (h d)") for c in range(4)])

            pe.wait_ge(rotated, 1)
            transpose_index("A")
            pe.wait_ge(rotated, 2)
            M = N_META
            transposes(("mT",), [r_i[0:M, 2, 4:6, :].rearrange("p h d -> p (h d)")]
                       + [r_k[0:M, 2, g, :, :].rearrange("p c d -> p (c d)") for g in range(KV)], M)

            def index_scores(t):
                for hd in range(IH):
                    half = slice(64 * (hd % 2), 64 * (hd % 2) + 64)
                    wait_free(pe, "is", t, hd)
                    if hd == 0 and t == 0:
                        wait_taken(pe, "mT")
                    full(pe.matmul(bank("is", t, hd)[:, 0:NK_OF[t]], iT[half, t, hd // 2, :],
                                   kiT[half, 0:NK_OF[t]], start=True, stop=True))

            pool_inputs()
            index_scores(0)
            pe.wait_ge(rotated, 3)
            transpose_queries(0)
            pe.wait_ge(rotated, 4)
            transpose_index("B")
            pe.wait_ge(rotated, 5)
            transposes(("kT",), [r_k[:, t, g, :, :].rearrange("p c d -> p (c d)") for t in range(TILES) for g in range(KV)])
            transpose_queries(1)

            def gates(c):
                name = f"g{c // 2}"
                wait_chunk(pe, name)
                wait_free(pe, "gate", c)
                for i in range(2):
                    col = (2 * (c % 2) + i) * P
                    for k in range(KD):
                        mm = pe.matmul(bank("gate", c)[:, i * SEQ:(i + 1) * SEQ].rearrange("p (t n) -> p t n", t=TILES),
                                       chunk(name, KD)[:, k, col:col + P], hT[:, :, k, N_META:N_META + P], start=(k == 0), stop=(k == KD - 1))
                full(mm)

            for c in range(3):
                gates(c)

            def attention_score(t, hd):
                half = slice(64 * (hd % 2), 64 * (hd % 2) + 64)
                wait_free(pe, "sc", t, hd)
                if hd == 0 and t == 0:
                    wait_taken(pe, "qT", 1)
                full(pe.matmul(bank("sc", t, hd)[:, 0:NK_OF[t]], qT[half, t, hd // 2, :],
                               kT[half, hd // 4, 0:NK_OF[t]], start=True, stop=True))

            def transpose_meta_probs(t, c):
                pe.wait_ge(probs_ready, t * HEADS + 4 * c + 4)
                wait_free(pe, "pm", t, c)
                for i in range(4):
                    mm = pe.transpose(bank("pm", t, c)[0:N_META, i * P:(i + 1) * P],
                                      probs[:, 4 * c + i, 0:N_META], ident[:, :])
                full(mm)

            def transpose_probs(t, c):
                per = 4 // (t + 1)
                wait_free(pe, "pk", t, c)
                for i in range(per):
                    for b in range(t + 1):
                        mm = pe.transpose(bank("pk", t, c)[:, (i * (t + 1) + b) * P:(i * (t + 1) + b + 1) * P],
                                          probs[:, c * per + i, POS[b]:POS[b] + P], ident[:, :])
                full(mm)

            def attend(t):
                wait_free(pe, "pv", t)
                wait_taken(pe, "pk", t, 2 * (t + 1) - 1)
                for hd in range(HEADS):
                    g = slice(64 * (hd // 4), 64 * (hd // 4) + 64)
                    o = bank("pv", t)[:, hd * DH:(hd + 1) * DH]
                    pe.matmul(o, pT_meta[0:N_META, hd, :], v_sb[0:N_META, 2, g], start=True, stop=False)
                    for b in range(t + 1):
                        mm = pe.matmul(o, pT[:, hd, b, :], v_sb[:, b, g], start=False, stop=(b == t))
                full(mm)

            def transpose_o(t):
                pe.wait_ge(o_ready, t + 1)
                transposes(("oT", t), [o_sb[:, 2 * c:2 * c + 2, :].rearrange("p h d -> p (h d)") for c in range(4)])

            def blocks(name, w, src, t, c, tiles, again=""):
                kk = src.shape[1]
                if tiles[0] == 0:
                    wait_chunk(pe, w + again)
                    wait_free(pe, name, t, c)
                for i in tiles:
                    col = (i if name == "ga" else 4 * c + i) * P
                    for k in range(kk):
                        mm = pe.matmul(bank(name, t, c)[:, i * P:(i + 1) * P], chunk(w + again, kk)[:, k, col:col + P],
                                       src[:, k, :], start=(k == 0), stop=(k == kk - 1))
                if tiles[-1] == 3:
                    full(mm)

            def output_products(t, products, again=""):
                for m in products:
                    c, k = m // KD, m % KD
                    if k == 0:
                        wait_chunk(pe, f"out{c}" + again)
                        pe.wait_ge(merged, 2 * t + 2)
                        wait_free(pe, "mx", t, c)
                    mm = pe.matmul(bank("mx", t, c)[:, :], gT[:, t, k, :], chunk(f"out{c}" + again, KD)[:, k, :],
                                   start=(k == 0), stop=(k == KD - 1))
                    if k == KD - 1:
                        full(mm)

            def transpose_h1(t):
                for c, ready in enumerate((ln_half, ln_done)):
                    pe.wait_ge(ready, 4 + t)
                    transposes(("h1T", t, c), [h[:, t, (4 * c + k) * P:(4 * c + k + 1) * P] for k in range(4)])

            def queries(t, n, which, again=""):
                if which[0] == 0:
                    wait_chunk(pe, f"wq{n // 4}" + again)
                    wait_free(pe, "q2", t, n)
                for i in which:
                    col = (n % 4 + i) * P
                    for k in range(KD):
                        if n == i == 0 and k % 4 == 0:
                            wait_taken(pe, "h1T", t, k // 4)
                        mm = pe.matmul(bank("q2", t, n)[:, i * P:(i + 1) * P],
                                       chunk(f"wq{n // 4}" + again, KD)[:, k, col:col + P], h1T[:, t, k, :],
                                       start=(k == 0), stop=(k == KD - 1))
                if which[-1] == dict(QUERY_BLOCKS[t])[n] - 1:
                    full(mm)

            def key_scores(t, n):
                wait_free(pe, "ss", t, n)
                wait_taken(pe, "q2", t, n)
                for i in range(dict(QUERY_BLOCKS[t])[n]):
                    mm = pe.matmul(bank("ss", t, n)[:, i * NK:(i + 1) * NK], q2T[:, t, n + i, :], keysT[:, n + i, :],
                                   start=True, stop=True)
                full(mm)

            def attention_gates(t, c, which):
                blocks("ga", f"g{2 + c}", hT[:, t, :, N_META:N_META + P], t, c, which)

            for hd in range(HEADS):
                attention_score(0, hd)
            gates(3)
            pe.wait_ge(windows_done, PG)
            for c in range(2):
                wait_free(pe, "yT", c)
                for i in range(2):
                    g = 2 * c + i
                    mm = pe.matmul(bank("yT", c)[:, i * SEQ:(i + 1) * SEQ], pw[:, g, :], xpT[:, g, N_META:NPOS],
                                   start=True, stop=True)
                full(mm)
            index_scores(1)
            wait_taken(pe, "yT", 1)
            for c in range(2):
                blocks("po", "pool_up", yT[:, 0, :, :], 0, c, range(4))
            for c in range(2):
                transpose_meta_probs(0, c)
            for c in range(2):
                transpose_probs(0, c)
            attention_gates(0, 0, range(4))
            attend(0)
            attention_gates(0, 1, range(4))
            transpose_o(0)

            def pool_output_b(which):
                for m in which:
                    blocks("po", "pool_up", yT[:, 1, :, :], 1, m // 4, [m % 4])

            pool_output_b([0])
            wait_taken(pe, "oT", 0)
            for c in range(2):
                blocks("ao", "attn_o", oT[:, 0, :, :], 0, c, range(4))
            pool_output_b([1, 2])
            output_products(0, range(2 * KD))
            pool_output_b(range(3, 8))
            transpose_h1(0)

            def give_slot(n):
                wait_full(pe, "q2", 0, n)
                pe.sem_inc(group_free, 1)

            pe.wait_ge(keys_in, 16)
            queries(0, 0, range(2))
            queries(0, 2, [0])
            key_scores(0, 0)
            queries(0, 2, [1])
            give_slot(2)
            queries(0, 4, range(4))
            give_slot(4)
            key_scores(0, 2)
            queries(0, 8, range(4))
            give_slot(8)
            key_scores(0, 4)
            queries(0, 12, range(4))
            give_slot(12)

            def add_residual(t, first):
                for c in range(2):
                    pe.matmul(Y[t][c][:, :], alpha_i[:, :], h[:, t, c * 512:(c + 1) * 512], start=first, stop=False,
                              skip_group_check=True)

            def beside(n):
                first, second = range(0, 2), range(2, 4)
                if n == 0:
                    key_scores(0, 8)
                    key_scores(0, 12)
                elif n < 5:
                    attention_score(1, 2 * n - 2)
                    attention_score(1, 2 * n - 1)
                elif n < 9:
                    attention_gates(1, 0, [n - 5])
                elif n == 9:
                    transpose_meta_probs(1, 0)
                    transpose_meta_probs(1, 1)
                elif n == 11:
                    transpose_probs(1, 0)
                    transpose_probs(1, 1)
                elif n == 12:
                    transpose_probs(1, 2)
                    transpose_probs(1, 3)
                elif n == 16:
                    attend(1)
                elif n in (14, 15, 17, 18):
                    attention_gates(1, 1, [(14, 15, 17, 18).index(n)])
                elif n == 20:
                    transpose_o(1)
                elif n == 22:
                    add_residual(0, False)
                elif 23 <= n < 27:
                    if n == 23:
                        wait_taken(pe, "oT", 1)
                    c, half = (n - 23) // 2, (n - 23) % 2
                    blocks("ao", "attn_o", oT[:, 1, :, :], 1, c, second if half else first, " again")
                elif 29 <= n < 35:
                    output_products(1, range(3 * (n - 29), min(3 * (n - 28), 2 * KD)), " again")
                elif n == 41:
                    transpose_h1(1)
                elif n in (42, 43):
                    pe.wait_ge(ln2_in, 16)
                    pe.wait_ge(ones_ready, 1)
                    for c in range(2 * (n - 42), 2 * (n - 41)):
                        wait_free(pe, "ln2", c)
                        full(pe.matmul(bank("ln2", c)[:, :], ones, ln2_row[:, c * 512:(c + 1) * 512],
                                       start=True, stop=True))
                elif n in (44, 49, 53, 58):
                    if n > 49:
                        key_scores(1, 4 * (44, 49, 53, 58).index(n) - 4)
                    queries(1, 4 * (44, 49, 53, 58).index(n), first, " again")
                elif n in (45, 50, 54, 59):
                    queries(1, 4 * (45, 50, 54, 59).index(n), second, " again")
                elif n == 48:
                    key_scores(1, 0)
                elif n == 62:
                    key_scores(1, 12)

            def unit(u, t, first=False, final=False, groups=GROUPS):
                for g, experts in groups:
                    pe.wait_ge(diag_ready, u * GPU + g + 1)
                    for e in experts:
                        for c in range(2):
                            last = final and e == EK - 1
                            mm = pe.matmul(Y[t][c][:, :], diag[:, e % RING, :], ring[:, e % RING, D + c * 512:D + (c + 1) * 512],
                                           start=first and e == 0, stop=last, skip_group_check=True)
                            if last and c == 0:
                                mm.then_inc(y_ready, 1)
                    mm.then_inc(group_free, 1)
                    if isinstance(u, int) and u < PH:
                        beside(u * GPU + g)

            for b in range(4, 8):
                wait_taken(pe, *JOBS[[m for m in range(len(JOBS)) if BANK_AT[m] == b][-1]][0])
            for u in range(PH):
                unit(u, 0, first=(u == 0), final=(u == PH - 1))
            add_residual(1, True)
            with pe.Fori(4, 7) as j:
                for b in range(2):
                    unit(2 * j + b, 1)
            unit(UNITS - 2, 1)
            unit(UNITS - 1, 1, final=True, groups=LAST_GROUPS)

        @block.vector
        def _(v):
            count = [0, 0]

            def link(i):
                count[0] += 1
                i.then_inc(dve_step, 1)
                v.wait_ge(dve_step, count[0])

            def step(i):
                count[0] += 1
                i.then_inc(dve_step, 1)

            def sync():
                v.wait_ge(dve_step, count[0])

            def half_stats(c, half, r):
                step(v.bn_stats(stats[0:r, c, :], half))

            def norm_begin(dst, halves, r, n):
                sync()
                link(v.bn_aggr(mv[0:r, :], stats[0:r, :, :].rearrange("p c n -> p (c n)")))
                v.tensor_scalar(nrm[0:r, 0:1], mv[0:r, 1:2], LN_EPS, None, ALU.add).then_inc(var_ready, 1)
                if n < 2:
                    v.wait_ge(ln_g_in[n], 16)
                else:
                    v.wait_ge(ln2_spread, 4)
                for c in range(2):
                    step(v.scalar_tensor_tensor(dst[:, c * 512:(c + 1) * 512], halves[c], mv[0:r, 0:1],
                                                ln_g[0:r, c * 512:(c + 1) * 512], ALU.subtract, ALU.mult))

            def norm_end(dst, r, n):
                count[1] += 1
                v.wait_ge(std_ready, count[1])
                link(v.reciprocal(nrm[0:r, 2:3], nrm[0:r, 1:2]))
                link(v.tensor_scalar(nrm[0:r, 3:4], nrm[0:r, 2:3], nrm[0:r, 2:3], nrm[0:r, 0:1], ALU.mult, ALU.mult))
                link(v.tensor_scalar(nrm[0:r, 4:5], nrm[0:r, 3:4], -0.5, 1.5, ALU.mult, ALU.add))
                link(v.tensor_scalar(nrm[0:r, 5:6], nrm[0:r, 4:5], nrm[0:r, 2:3], None, ALU.mult))
                if n < 2:
                    v.wait_ge(ln_b_in[n], 16)
                for c, ready in enumerate((ln_half, ln_done)):
                    cols = slice(c * 512, (c + 1) * 512)
                    v.scalar_tensor_tensor(dst[:, cols], dst[:, cols], nrm[0:r, 5:6], ln_b[0:r, cols], ALU.mult,
                                           ALU.add).then_inc(ready, 1)
                v.wait_ge(ln_half, count[1])
                v.wait_ge(ln_done, count[1])

            def layer_norm(dst, halves, r, n):
                for c in range(2):
                    half_stats(c, halves[c], r)
                norm_begin(dst, halves, r, n)
                norm_end(dst, r, n)

            v.memset(arena[:, 0:512], 0.0).then_inc(zeros_ready, 1)
            v.memset(hT[:, 1, :, 0:N_META], 0.0).then_inc(pad_ready, 1)
            link(v.memset(nrm[:, :], 1.0))
            for t in "AMB":
                n, r = rows[t]
                v.wait_ge(x_in[n], 16)
                src = h_meta if t == "M" else h[:, n, :]
                layer_norm(src, [src[:, 0:512], src[:, 512:1024]], r, 0)

            def rope(src, dst, tab, r, hh, half):
                w = 2 * half
                t2 = tmp[0:r, 0:hh * w].rearrange("p (h d) -> p h d", h=hh)
                cos = tab[:, 0, :].unsqueeze(1).broadcast_to([r, hh, w])
                sin = tab[:, 1, :].unsqueeze(1).broadcast_to([r, hh, w])
                step(v.tensor_tensor(dst[:, :, 0:w], src[:, :, 0:w], cos, ALU.mult))
                step(v.tensor_tensor(t2[:, :, 0:half], src[:, :, half:w], sin[:, :, 0:half], ALU.mult))
                link(v.tensor_tensor(t2[:, :, half:w], src[:, :, 0:half], sin[:, :, half:w], ALU.mult))
                link(v.tensor_tensor(dst[:, :, 0:w], dst[:, :, 0:w], t2, ALU.add))

            v.wait_ge(const_in, 16 * N_CONST)

            def rope_index(n, r, src):
                hh = src.shape[1]
                dst = r_i[0:r, n, 5 - hh:5, :]
                step(v.tensor_copy(dst[:, :, 32:64], src[:, :, 32:64]))
                rope(src, dst, tabs_i[0:r, n, :, :], r, hh, 16)
                return v.tensor_copy(r_i[0:r, n, 5, :], r_i[0:r, n, 4, :])

            def rope_tile_index(t, nth):
                n, r = rows[t]
                wait_taken(v, "zs", t)
                rope_index(n, r, z[:, n, OFF_QI:OFF_QI + 320].rearrange("p (h d) -> p h d", d=DH)).then_inc(rotated, 1)
                v.wait_ge(rotated, nth)

            def rope_tile(t, nth):
                n, r = rows[t]
                wait_taken(v, "zq", t)
                rope(z[:, n, 0:640].rearrange("p (h d) -> p h d", d=DH), r_qk[:, n, :, :], tabs_q[:, n, :, :], r, 10, 32)
                v.tensor_copy(r_k[:, n, :, :, :], r_qk[:, n, 8:10, :].unsqueeze(2).broadcast_to([P, KV, 2, DH])).then_inc(rotated, 1)
                v.wait_ge(rotated, nth)

            rope_tile_index("A", 1)
            wait_taken(v, "zs", "M")
            M = N_META
            link(rope_index(2, M, z_m[0:M, 256:320].rearrange("p (h d) -> p h d", d=DH)))
            rope(z_m[0:M, 0:128].rearrange("p (h d) -> p h d", d=DH), r_mk[0:M, :, :], tabs_q[0:M, 2, :, :], M, KV, 32)
            v.tensor_copy(r_k[0:M, 2, :, :, :], r_mk[0:M, :, :].unsqueeze(2).broadcast_to([M, KV, 2, DH])).then_inc(rotated, 1)
            v.wait_ge(rotated, 2)
            rope_tile("A", 3)
            rope_tile_index("B", 4)
            rope_tile("B", 5)

            def select_keys(t):
                n = NK_OF[t]
                acc, left = isum[:, 0, 0:n], isum[:, 1, 0:n]
                mask = causal[:, t, 0:n]
                for hd in range(IH):
                    wait_full(v, "is", t, hd)
                    dst = rel[:, 0:n] if hd else acc
                    v.tensor_scalar(dst, bank("is", t, hd)[:, 0:n], 0.0, wi[:, t, hd:hd + 1], ALU.max,
                                    ALU.mult).then_inc(bank_taken["dve"], 1)
                    wait_taken(v, "is", t, hd)
                    if hd:
                        link(v.tensor_tensor(acc, acc, rel[:, 0:n], ALU.add))
                link(v.tensor_tensor(acc, acc, mask, ALU.add))
                cur, other = acc, left
                for _ in range(TOPK // 8):
                    link(v.max(m8[:, :], cur))
                    link(v.match_replace(other, m8[:, :], cur, NEG_TAKEN))
                    cur, other = other, cur
                link(v.tensor_scalar(cur, cur, -3.2e38, MASK, ALU.is_le, ALU.mult))
                link(v.tensor_scalar(mask, mask, -MASK / NEG_CAUSAL, -MASK, ALU.mult, ALU.add))
                link(v.tensor_tensor(mask, mask, cur, ALU.add))

            def softmax_input(t, hd):
                n = NK_OF[t]
                if hd == 0:
                    wait_full(v, *(("oT", 0) if t else ("qT", 1)))
                wait_full(v, "sc", t, hd)
                v.tensor_tensor_reduce(probs[:, hd, 0:n], bank("sc", t, hd)[:, 0:n], causal[:, t, 0:n], -SCALE, 3.0e38,
                                       ALU.add, ALU.min, neg_max[:, hd:hd + 1]).then_inc(bank_taken["dve"], 1)
                wait_taken(v, "sc", t, hd)
                v.sem_inc(scored, 1)

            def normalise(t):
                v.wait_ge(probs_ready, (t + 1) * HEADS)
                link(v.reciprocal(row_inv[:, :], row_sum[:, :]))
                wait_full(v, "pv", t)
                v.tensor_tensor(o_sb[:, :, :], bank("pv", t)[:, :].rearrange("p (h d) -> p h d", h=HEADS),
                                row_inv[:, :].unsqueeze(2).broadcast_to([P, HEADS, DH]), ALU.mult).then_inc(bank_taken["dve"], 1)
                wait_taken(v, "pv", t)
                v.sem_inc(o_ready, 1)

            def gate_pool(t, c):
                wait_full(v, "po", t, c)
                g = gT[:, t, 4 * c:4 * c + 4, :].rearrange("p c n -> p (c n)")
                v.tensor_tensor(g, g, bank("po", t, c)[:, :], ALU.mult).then_inc(bank_taken["dve"], 1)

            def gate_attention(t, c):
                wait_full(v, "ao", t, c)
                wait_taken(v, "ga", t, c)
                g = gT[:, t, KD + 4 * c:KD + 4 * c + 4, :].rearrange("p c n -> p (c n)")
                v.tensor_tensor(g, g, bank("ao", t, c)[:, :], ALU.mult).then_inc(bank_taken["dve"], 1)
                wait_taken(v, "ao", t, c)
                m = gT[:, t, 4 * c:4 * c + 4, :].rearrange("p c n -> p (c n)")
                v.tensor_tensor(m, m, g, ALU.add).then_inc(merged, 1)

            def residual(t, c):
                wait_full(v, "mx", t, c)
                hh = h[:, t, c * 512:(c + 1) * 512]
                v.scalar_tensor_tensor(hh, hh, ALPHA, bank("mx", t, c)[:, :], ALU.mult, ALU.add).then_inc(bank_taken["dve"], 1)
                wait_taken(v, "mx", t, c)

            def halves_of(t):
                return [h[:, t, c * 512:(c + 1) * 512] for c in range(2)]

            select_keys(0)
            for hd in range(HEADS):
                softmax_input(0, hd)
            select_keys(1)
            wait_taken(v, "gate", 3)
            for c in range(2):
                gate_pool(0, c)
            normalise(0)
            for c in range(2):
                gate_attention(0, c)
            for c in range(2):
                residual(0, c)
                half_stats(c, halves_of(0)[c], P)
            norm_begin(h[:, 0, :], halves_of(0), P, 1)
            norm_end(h[:, 0, :], P, 1)
            for c in range(2):
                gate_pool(1, c)

            def topk(u, b):
                n = [0]

                def sig(i):
                    n[0] += 1
                    i.then_inc(topk_step, 1)

                def need(k):
                    v.wait_ge(topk_step, u * TOPK_STEPS + k)
                    if not isinstance(u, int):
                        v.sem_inc(dve_passed, 1)

                v.wait_ge(s_loaded, u + 1)
                if not isinstance(u, int):
                    v.sem_inc(dve_passed, 1)
                S = [s_cur[:, b, c, :] for c in range(2)]
                for c in range(2):
                    sig(v.max(top_v[:, c, 0:8], S[c]))
                for c in range(2):
                    need(1 + c)
                    sig(v.max_index(top_i[:, c, 0:8], top_v[:, c, 0:8], S[c]))
                for c in range(2):
                    sig(v.match_replace(s_left[:, c, :], top_v[:, c, 0:8], S[c], NEG_TAKEN))
                yield
                for c in range(2):
                    need(5 + c)
                    sig(v.max(top_v[:, c, 8:16], s_left[:, c, :]))
                for c in range(2):
                    need(7 + c)
                    sig(v.max_index(top_i[:, c, 8:16], top_v[:, c, 8:16], s_left[:, c, :]))
                sig(v.tensor_tensor(cand[:, :, :], top_v[:, 0, :].unsqueeze(2).broadcast_to([P, EK, EK]),
                                    top_v[:, 1, :].unsqueeze(1).broadcast_to([P, EK, EK]), ALU.add))
                flat = cand[:, :, :].rearrange("p a b -> p (a b)")
                need(11)
                sig(v.tensor_copy(top_if[:, :, :], top_i[:, :, :]))
                yield
                sig(v.max(best[:, b, 0:8], flat))
                need(13)
                sig(v.max_index(sel[:, 0:8], best[:, b, 0:8], flat))
                sig(v.match_replace(cand2[:, :], best[:, b, 0:8], flat, NEG_TAKEN))
                need(15)
                sig(v.max(best[:, b, 8:16], cand2[:, :]))
                need(16)
                sig(v.max_index(sel[:, 8:16], best[:, b, 8:16], cand2[:, :]))
                v.tensor_scalar(neg_top[:, b:b + 1], best[:, b, 0:1], -1.0, None, ALU.mult).then_inc(top_ready, 1)
                yield
                v.wait_ge(topk_step, u * TOPK_STEPS + 17)
                sig(v.tensor_scalar(ab[:, 0, :], sel[:, :], 4, None, ALU.logical_shift_right))
                sig(v.tensor_scalar(ab[:, 1, :], sel[:, :], 15, None, ALU.bitwise_and))
                v.wait_ge(topk_step, u * TOPK_STEPS + 19)
                sig(v.tensor_copy(abf[:, :, :], ab[:, :, :]))
                v.wait_ge(topk_step, u * TOPK_STEPS + 20)
                for c in range(2):
                    sig(v.tensor_tensor(hot[:, c, :, :], abf[:, c, :].unsqueeze(2).broadcast_to([P, EK, EK]),
                                        iota16[:, :].unsqueeze(1).broadcast_to([P, EK, EK]), ALU.is_equal))
                for c in range(2):
                    v.wait_ge(topk_step, u * TOPK_STEPS + 21 + c)
                    sig(v.tensor_tensor(hot[:, c, :, :], hot[:, c, :, :],
                                        top_if[:, c, :].unsqueeze(1).broadcast_to([P, EK, EK]), ALU.mult))
                yield
                v.wait_ge(topk_step, u * TOPK_STEPS + 24)
                v.tensor_reduce(pick[:, :, :], hot[:, :, :, :], AX_X, ALU.add).then_inc(pick_ready, 1)
                v.wait_ge(pick_ready, u + 1)
                v.scalar_tensor_tensor(expert[:, b, :], pick[:, 0, :], float(NK), pick[:, 1, :], ALU.mult,
                                       ALU.add).then_inc(idx_ready, 1)
                assert n[0] == TOPK_STEPS

            def unit(u, t, b, nxt, groups=GROUPS):
                v.wait_ge(gexp_ready, u + 1)
                v.reciprocal(ginv[:, b:b + 1], gsum[:, b:b + 1]).then_inc(gate_ready, 1)
                v.wait_ge(gate_ready, 2 * u + 1)
                v.tensor_scalar(gate[:, b, :], gexp[:, b, :], ginv[:, b:b + 1], None, ALU.mult).then_inc(gate_ready, 1)
                v.wait_ge(gate_ready, 2 * u + 2)
                best_of = topk(u + 2, b) if nxt else iter(())
                for g, experts in groups:
                    for e in experts:
                        v.wait_ge(landed[e % RING], 16 * (u * (EK // RING) + e // RING + 1))
                        u_row = ring[:, e % RING, 0:D]
                        d = v.tensor_tensor_reduce(u_row, u_row, h[:, t, :], 1.0, 0.0, ALU.mult, ALU.add, dot[:, b, e:e + 1])
                    d.then_inc(dots_ready, 1)
                    v.wait_ge(gelu_ready, u * GPU + g + 1)
                    e = slice(experts[0], experts[-1] + 1)
                    v.tensor_tensor(w_e[:, b, e], act_e[:, b, e], gate[:, b, e], ALU.mult).then_inc(w_ready, 1)
                    if g > LOAD_AT:
                        next(best_of, None)
                    if isinstance(u, int) and u < PH:
                        beside(u * GPU + g)
                    if isinstance(u, int) and u == UNITS - 2:
                        last_norm_of_a(g)

            def last_norm_of_a(g):
                halves = [Y[0][c][:, :] for c in range(2)]
                if g == 0:
                    v.wait_ge(group_free, AHEAD + PH * GPU)
                    for c in range(2):
                        half_stats(c, halves[c], P)
                    norm_begin(h[:, 0, :], halves, P, 2)
                if g == 2:
                    norm_end(h[:, 0, :], P, 2)

            def beside(n):
                if 3 <= n < 7:
                    softmax_input(1, 2 * (n - 3))
                    softmax_input(1, 2 * (n - 3) + 1)
                if n == 18:
                    normalise(1)
                if n in (26, 28):
                    gate_attention(1, (n - 26) // 2)
                if n in (33, 36):
                    c = (n - 33) // 3
                    residual(1, c)
                    half_stats(c, halves_of(1)[c], P)
                if n == 36:
                    norm_begin(h[:, 1, :], halves_of(1), P, 1)
                if n == 38:
                    norm_end(h[:, 1, :], P, 1)
                    v.memset(ones, 1.0).then_inc(ones_ready, 1)

            for b in range(2):
                for _ in topk(b, b):
                    pass

            for u in range(PH):
                unit(u, 0, u % 2, True)
            with v.Fori(4, 7) as j:
                for b in range(2):
                    unit(2 * j + b, 1, b, True)
            unit(UNITS - 2, 1, 0, False)
            unit(UNITS - 1, 1, 1, False, LAST_GROUPS)
            halves = [Y[1][c][:, :] for c in range(2)]
            for c in range(2):
                if c == 0:
                    v.wait_ge(y_ready, 2)
                else:
                    v.wait_ge(group_free, AHEAD + UNITS * GPU + 1)
                half_stats(c, halves[c], P)
            norm_begin(h[:, 1, :], halves, P, 2)
            norm_end(h[:, 1, :], P, 2)


def kernel(**inputs):
    import concourse.bacc as bacc
    from concourse.bass_utils import run_bass_kernel_spmd as run

    a = {k: np.asarray(v) for k, v in inputs.items()}
    nc = bacc.Bacc("TRN2", target_bir_lowering=False, num_devices=1)
    arrays, aps = {}, {}

    def give(name, value):
        value = np.ascontiguousarray(value)
        arrays[name] = value
        aps[name] = nc.dram_tensor(name, value.shape, mybir.dt.from_np(value.dtype), kind="ExternalInput").ap()

    def tables(rot):
        half = rot // 2
        inv = np.float32(10000.0) ** (-np.arange(half, dtype=np.float32) / np.float32(half))
        ang = np.arange(NPOS, dtype=np.float32)[:, None] * inv[None, :].astype(np.float32)
        cos, sin = np.cos(ang), np.sin(ang)
        return np.stack([np.concatenate([cos, cos], 1), np.concatenate([-sin, sin], 1)], 1).astype(np.float32)

    give("x", a["x"][0])
    give("meta", a["meta_tokens"])
    give("ln", np.stack([a["ln0_g"], a["ln0_b"], a["ln1_g"][0], a["ln1_b"][0], a["ln2_g"][0], a["ln2_b"][0]]))
    give("w_in", a["w_in"][0])
    give("b_gate_t", a["b_gate"][0].reshape(2 * KD, P).T)
    give("pool_w", a["pool_w"][0])
    give("pool_scale_t", a["pool_scale"][0].reshape(PG, P).T)
    give("w_pool_up", a["w_pool_up"][0])
    give("w_attn_o", a["w_attn_o"][0])
    give("w_out", a["w_out"][0])
    give("wq", a["peer_wq"][0])
    give("keys_t", a["peer_sub_keys"][0].reshape(2 * PH, NK, P).transpose(2, 0, 1))
    give("uv", np.concatenate([a["peer_u"][0], a["peer_v"][0]], axis=1))
    give("rope_q", tables(DH))
    give("rope_i", tables(32))
    give("ident_in", np.eye(P, dtype=np.float32))
    give("alpha_in", (np.eye(P) * ALPHA).astype(np.float32))
    give("iota_in", np.tile(np.arange(EK, dtype=np.float32), (P, 1)))
    q_pos = N_META + np.arange(SEQ)
    give("causal_in", np.where(np.arange(NPOS)[None, :] <= q_pos[:, None], 0.0, NEG_CAUSAL).astype(np.float32))
    out = nc.dram_tensor("out", (1, SEQ, D), F32, kind="ExternalOutput").ap()
    layer_kernel(nc, *aps.values(), out)
    r = run(nc, [arrays], core_ids=[0])
    return r.results[0]["out"]
```
